# Optimizing a Trainium2 kernel written in Bass

```python
import math
import jax
import jax.numpy as jnp
from jax import lax
import numpy as np

D_MODEL = 1024
BATCH = 1
SEQ = 256
DEPTH = 2

N_A = DEPTH // 2
N_B = DEPTH - N_A
CONV_W = 3
D_FF = 2816
N_HEADS = 16
N_KV_GROUPS = 4
HPG = N_HEADS // N_KV_GROUPS
HEAD_DIM = 64
CMP_LEN = 32
CMP_STRIDE = 16
CMP_HIDDEN = 128
SLC_LEN = 64
N_SEL = 16
WINDOW = 512
Q_BLOCK = 128
BAND = WINDOW + Q_BLOCK
N_BUCKETS = 32
MAX_DISTANCE = 128
N_KV_SLOTS = 6
EPS = 1e-6
NEG = -1e30

kernel_name = 'yoco_shortconv_nsa_hybrid'

def rmsnorm(x, g):
    xf = x.astype(jnp.float32)
    y = xf * lax.rsqrt(jnp.mean(xf * xf, axis=-1, keepdims=True) + EPS)
    return (y * g.astype(jnp.float32)).astype(x.dtype)

def causal_dwconv(u, w):
    s = u.shape[1]
    up = jnp.pad(u, ((0, 0), (CONV_W - 1, 0), (0, 0)))
    return sum(up[:, k:k + s] * w[k] for k in range(CONV_W))

def rel_bucket(dist):
    max_exact = N_BUCKETS // 2
    d = jnp.maximum(dist, 0)
    df = jnp.maximum(d, 1).astype(jnp.float32)
    large = max_exact + (jnp.log(df / max_exact) / math.log(MAX_DISTANCE / max_exact)
                         * (N_BUCKETS - max_exact)).astype(jnp.int32)
    return jnp.where(d < max_exact, d, jnp.minimum(large, N_BUCKETS - 1))

def short_conv_mixer(h, w_in, conv_w, w_out):
    bg, cg, v = jnp.split(h @ w_in, 3, axis=-1)
    return (bg * causal_dwconv(cg * v, conv_w)) @ w_out

def conv_ffn(h, w_up, conv_w, w_down):
    u = causal_dwconv(h @ w_up, conv_w)
    a, g = jnp.split(u, 2, axis=-1)
    return (jax.nn.silu(a) * g) @ w_down

def nsa_shared_kv(s, w_kv, cmp_pe, cmp_w1, cmp_b1, cmp_w2):
    b, n, _ = s.shape
    kv = (s @ w_kv).reshape(b, n, N_KV_SLOTS, N_KV_GROUPS, HEAD_DIM)
    n_c = (n - CMP_LEN) // CMP_STRIDE + 1
    n_s = n // SLC_LEN
    idx = (jnp.arange(n_c) * CMP_STRIDE)[:, None] + jnp.arange(CMP_LEN)[None, :]

    def compress(tok, j):
        blk = tok[:, idx] + cmp_pe[j][None, None, :, None, :]
        blk = blk.transpose(0, 1, 3, 2, 4).reshape(b, n_c, N_KV_GROUPS, CMP_LEN * HEAD_DIM)
        return jax.nn.gelu(blk @ cmp_w1[j] + cmp_b1[j]) @ cmp_w2[j]

    k_cmp = compress(kv[:, :, 0], 0)
    v_cmp = compress(kv[:, :, 1], 1)
    k_slc = kv[:, :, 2].reshape(b, n_s, SLC_LEN, N_KV_GROUPS, HEAD_DIM)
    v_slc = kv[:, :, 3].reshape(b, n_s, SLC_LEN, N_KV_GROUPS, HEAD_DIM)
    pad = ((0, 0), (WINDOW, 0), (0, 0), (0, 0))
    k_win = jnp.pad(kv[:, :, 4], pad)
    v_win = jnp.pad(kv[:, :, 5], pad)
    return (k_cmp, v_cmp, k_slc, v_slc, k_win, v_win)

def nsa_query_block(q, gate, qs, k_cmp, v_cmp, k_slc, v_slc, k_win, v_win, rel_bias, overlap):
    t_len = q.shape[0]
    n_c = k_cmp.shape[0]
    n_s = k_slc.shape[0]
    n_sel = min(N_SEL, n_s)
    garr = jnp.arange(N_KV_GROUPS)
    tb = rel_bias.astype(jnp.float32).reshape(N_BUCKETS, N_KV_GROUPS, HPG)
    qg = (q * HEAD_DIM ** -0.5).reshape(t_len, N_KV_GROUPS, HPG, HEAD_DIM).transpose(1, 2, 0, 3)
    t_pos = qs + jnp.arange(t_len)

    c_end = jnp.arange(n_c) * CMP_STRIDE + (CMP_LEN - 1)
    dist_c = t_pos[:, None] - c_end[None, :]
    mask_c = dist_c >= 0
    bias_c = tb[rel_bucket(dist_c)].transpose(2, 3, 0, 1)
    s_c = jnp.einsum('ghtd,cgd->ghtc', qg, k_cmp).astype(jnp.float32) + bias_c
    p_c = jax.nn.softmax(jnp.where(mask_c, s_c, NEG), axis=-1) * mask_c
    o_c = jnp.einsum('ghtc,cgd->ghtd', p_c.astype(v_cmp.dtype), v_cmp)

    imp = jnp.einsum('ghtc,cs->gts', p_c, overlap)
    cur = t_pos // SLC_LEN
    jb = jnp.arange(n_s)[None, :]
    forced = (jb == 0) | (jb == cur[:, None]) | (jb == cur[:, None] - 1)
    score = jnp.where(forced, jnp.inf, jnp.where(jb <= cur[:, None], imp, -jnp.inf))
    _, sel = lax.top_k(score, n_sel)
    key_pos = sel[..., None] * SLC_LEN + jnp.arange(SLC_LEN)
    dist_s = t_pos[None, :, None, None] - key_pos
    mask_s = dist_s >= 0
    ks = k_slc.transpose(2, 0, 1, 3)[garr[:, None, None], sel]
    vs = v_slc.transpose(2, 0, 1, 3)[garr[:, None, None], sel]
    bias_s = jnp.moveaxis(tb[rel_bucket(dist_s), garr[:, None, None, None]], -1, 1)
    s_s = jnp.einsum('ghtd,gtnld->ghtnl', qg, ks).astype(jnp.float32) + bias_s
    s_s = jnp.where(mask_s[:, None], s_s, NEG)
    p_s = jax.nn.softmax(s_s.reshape(N_KV_GROUPS, HPG, t_len, -1), axis=-1).reshape(s_s.shape)
    o_s = jnp.einsum('ghtnl,gtnld->ghtd', p_s.astype(vs.dtype), vs)

    kw = lax.dynamic_slice_in_dim(k_win, qs, BAND, axis=0)
    vw = lax.dynamic_slice_in_dim(v_win, qs, BAND, axis=0)
    key_pos_w = qs - WINDOW + jnp.arange(BAND)
    dist_w = t_pos[:, None] - key_pos_w[None, :]
    mask_w = (dist_w >= 0) & (dist_w < WINDOW) & (key_pos_w[None, :] >= 0)
    bias_w = tb[rel_bucket(dist_w)].transpose(2, 3, 0, 1)
    s_w = jnp.einsum('ghtd,kgd->ghtk', qg, kw).astype(jnp.float32) + bias_w
    p_w = jax.nn.softmax(jnp.where(mask_w, s_w, NEG), axis=-1)
    o_w = jnp.einsum('ghtk,kgd->ghtd', p_w.astype(vw.dtype), vw)

    g = gate.reshape(t_len, N_KV_GROUPS, HPG, 3).transpose(1, 2, 0, 3)
    o = g[..., 0:1] * o_c + g[..., 1:2] * o_s + g[..., 2:3] * o_w
    return o.transpose(2, 0, 1, 3).reshape(t_len, N_HEADS * HEAD_DIM)

def nsa_mixer(h, w_qg, w_o, kv, rel_bias):
    b, n, _ = h.shape
    k_cmp, v_cmp, k_slc, v_slc, k_win, v_win = kv
    n_c = k_cmp.shape[1]
    n_s = k_slc.shape[1]
    nq = n // Q_BLOCK
    c_start = jnp.arange(n_c)[:, None] * CMP_STRIDE
    s_start = jnp.arange(n_s)[None, :] * SLC_LEN
    overlap = ((c_start < s_start + SLC_LEN) & (c_start + CMP_LEN > s_start)).astype(jnp.float32)
    hd = N_HEADS * HEAD_DIM
    qg = h @ w_qg
    q = qg[..., :hd].reshape(b * nq, Q_BLOCK, N_HEADS, HEAD_DIM)
    gate = jax.nn.sigmoid(qg[..., hd:]).reshape(b * nq, Q_BLOCK, N_HEADS, 3)
    b_idx = jnp.repeat(jnp.arange(b), nq)
    q_start = jnp.tile(jnp.arange(nq) * Q_BLOCK, b)

    def step(args):
        qb, gb, bi, qs = args
        return nsa_query_block(qb, gb, qs, k_cmp[bi], v_cmp[bi], k_slc[bi], v_slc[bi],
                               k_win[bi], v_win[bi], rel_bias, overlap)

    o = lax.map(step, (q, gate, b_idx, q_start))
    return o.reshape(b, n, hd) @ w_o

def setup_inputs(seed: int = 0) -> dict:
    key = jax.random.key(seed)
    k = jax.random.split(key, 20)

    def nrm(kk, shape, scale):
        return jax.random.normal(kk, shape, jnp.float32) * scale

    def gain(kk, shape):
        return 1.0 + 0.02 * jax.random.normal(kk, shape, jnp.float32)

    d, f, hd = D_MODEL, D_FF, N_HEADS * HEAD_DIM
    return {
        'x': nrm(k[0], (BATCH, SEQ, d), 1.0),
        'mix_norm': gain(k[1], (DEPTH, d)),
        'a_w_in': nrm(k[2], (N_A, d, 3 * d), d ** -0.5),
        'a_conv': nrm(k[3], (N_A, CONV_W, d), CONV_W ** -0.5),
        'a_w_out': nrm(k[4], (N_A, d, d), d ** -0.5),
        'ffn_norm': gain(k[5], (DEPTH, d)),
        'ffn_up': nrm(k[6], (DEPTH, d, 2 * f), d ** -0.5),
        'ffn_conv': nrm(k[7], (DEPTH, CONV_W, 2 * f), CONV_W ** -0.5),
        'ffn_down': nrm(k[8], (DEPTH, f, d), f ** -0.5),
        'kv_norm': gain(k[9], (d,)),
        'w_kv': nrm(k[10], (d, N_KV_SLOTS * N_KV_GROUPS * HEAD_DIM), d ** -0.5),
        'cmp_pe': nrm(k[11], (2, CMP_LEN, HEAD_DIM), 0.1),
        'cmp_w1': nrm(k[12], (2, CMP_LEN * HEAD_DIM, CMP_HIDDEN), (CMP_LEN * HEAD_DIM) ** -0.5),
        'cmp_b1': nrm(k[13], (2, CMP_HIDDEN), 0.02),
        'cmp_w2': nrm(k[14], (2, CMP_HIDDEN, HEAD_DIM), CMP_HIDDEN ** -0.5),
        'b_w_qg': nrm(k[15], (N_B, d, hd + 3 * N_HEADS), d ** -0.5),
        'b_w_o': nrm(k[16], (N_B, hd, d), hd ** -0.5),
        'rel_bias': nrm(k[17], (N_BUCKETS, N_HEADS), 0.5),
        'final_norm': gain(k[18], (d,)),
    }

def reference(x, mix_norm, a_w_in, a_conv, a_w_out, ffn_norm, ffn_up, ffn_conv, ffn_down,
              kv_norm, w_kv, cmp_pe, cmp_w1, cmp_b1, cmp_w2, b_w_qg, b_w_o, rel_bias, final_norm):
    kv = None
    for layer in range(DEPTH):
        if layer < N_A:
            i = layer
            x = x + short_conv_mixer(rmsnorm(x, mix_norm[layer]), a_w_in[i], a_conv[i], a_w_out[i])
        else:
            i = layer - N_A
            if layer == N_A:
                kv = nsa_shared_kv(rmsnorm(x, kv_norm), w_kv, cmp_pe, cmp_w1, cmp_b1, cmp_w2)
            x = x + nsa_mixer(rmsnorm(x, mix_norm[layer]), b_w_qg[i], b_w_o[i], kv, rel_bias)
        x = x + conv_ffn(rmsnorm(x, ffn_norm[layer]), ffn_up[layer], ffn_conv[layer], ffn_down[layer])
    return rmsnorm(x, final_norm)


_drawn_inputs = setup_inputs


def setup_inputs(seed=0):
    import zlib

    import numpy as np

    out = dict(_drawn_inputs(seed))
    spreads = {}
    factors = {'ffn_norm': 3.358, 'kv_norm': 8.0, 'cmp_pe': 11.04, 'cmp_b1': 47.85, 'final_norm': 8.418}
    for name, (base, spread) in spreads.items():
        noise = np.random.default_rng([zlib.crc32(name.encode()), seed]).standard_normal(out[name].shape)
        drawn = base * np.exp(spread * noise) if base else spread * noise
        out[name] = jnp.asarray(drawn.astype(out[name].dtype))
    for name, factor in factors.items():
        out[name] = (out[name] * factor).astype(out[name].dtype)
    return out
```

```python
import math
from contextlib import ExitStack

import numpy as np

import concourse.bass as bass
from concourse import mybir

ALU = mybir.AluOpType
ACT = mybir.ActivationFunctionType
F32 = mybir.dt.float32
F32R = mybir.dt.float32r

P = 128
D = 1024
T = 256
KT = D // P
F = 2816
FU = F // P
AU = D // P
HEADS = 16
GROUPS = 4
HPG = HEADS // GROUPS
HD = 64
CL, CS = 32, 16
NC = (T - CL) // CS + 1
BUCKETS = 32
MAXD = 128
EPS = 1e-6
NEG = -1e30
PW = 1024

PAR = {}
_at = 0
for _name, _n in (("gains", 6 * KT), ("a_taps", 3 * AU), ("f_taps", 2 * 2 * FU * 3), ("pe", 2 * 16),
                  ("b1", 2), ("w2", 2 * HD)):
    PAR[_name] = _at
    _at += _n
NPAR = _at
GAIN = {"mix0": 0, "ffn0": 1, "kv": 2, "mix1": 3, "ffn1": 4, "final": 5}

B_ORDER = ([("cmp", t) for t in range(4)] + [("key", t) for t in range(4)] + [("val", t) for t in range(4)]
           + [("w1", 0), ("w1", 1), ("gate", 0), ("q", 0), ("q", 1), ("w1", 2), ("w1", 3)]
           + [("q", t) for t in range(2, 8)])
NB = len(B_ORDER)
UP_SLOTS, DOWN_SLOTS = 6, 3


def plan_pieces():
    order = [("a", "up", u, c) for u in range(AU) for c in range(3)]
    order += [("f0", "up", u, c) for u in range(FU) for c in range(2)]
    order += [("b", "up", b, 0) for b in range(NB)]
    order += [("f1", "up", u, c) for u in range(FU) for c in range(2)]
    downs = [("a", "down", u, 0) for u in range(AU)] + [("f0", "down", u, 0) for u in range(FU)]
    downs += [("o", "down", u, 0) for u in range(8)] + [("f1", "down", u, 0) for u in range(FU)]
    table = {}
    for keys in (order, downs):
        used, turns = {}, {}
        for n, key in enumerate(keys):
            st, kind, u, c = key
            if kind == "up":
                slot = {"a": 3 * (u % 2) + c, "b": (u + 2) % 6}.get(st, 2 * (u % 3) + c)
            else:
                slot = UP_SLOTS + (u % 2 if st == "a" else u % 3)
            turns[slot] = turns.get(slot, 0) + 1
            table[key] = dict(n=n, slot=slot, turn=turns[slot], prev=used.get(slot))
            used[slot] = n
    return table


def bucket_of(dist):
    half = BUCKETS // 2
    if dist < half:
        return dist
    large = half + int(np.float32(np.log(np.float32(dist) / np.float32(half))) / np.float32(math.log(MAXD / half))
                       * np.float32(BUCKETS - half))
    return min(large, BUCKETS - 1)


def one_hot_of_distances():
    hot = np.zeros((BUCKETS + 1, 512), np.float32)
    for m in range(511):
        hot[bucket_of(255 - m) if m <= 255 else BUCKETS, m] = 1.0
    return hot


def build(nc, xT, par, hot, rel, a_up, a_down, f_up, f_down, b_up, b_down, scratch, out):
    piece = plan_pieces()
    ctx = ExitStack()
    with ctx:
        def sb(name, shape, dt=F32):
            return ctx.enter_context(nc.sbuf_tensor(name, shape, dt))

        def sem(name):
            return ctx.enter_context(nc.semaphore(name))

        x = sb("x", [P, KT, T])
        gx_hi = sb("gx_hi", [P, KT, T], F32R)
        gx_lo = sb("gx_lo", [P, KT, T], F32R)
        gq_hi = sb("gq_hi", [P, KT, T], F32R)
        gq_lo = sb("gq_lo", [P, KT, T], F32R)
        w_hi = sb("w_hi", [P, UP_SLOTS + DOWN_SLOTS, PW], F32R)
        w_lo = sb("w_lo", [P, UP_SLOTS + DOWN_SLOTS, PW], F32R)
        staged = sb("staged", [P, UP_SLOTS + 1, PW])
        bias = sb("bias", [P, HEADS, T])
        bias_c = sb("bias_c", [P, 2, HEADS, NC])
        y_hi = sb("y_hi", [P, 16 * 4 * NC], F32R)
        y_lo = sb("y_lo", [P, 16 * 4 * NC], F32R)
        params = sb("params", [P, NPAR])
        rstd = sb("rstd", [P, T])
        sumsq = sb("sumsq", [P, 2, T])
        ones = sb("ones", [P, P])
        ident = sb("ident", [P, P])
        flip = sb("flip", [P, P])
        eps = sb("eps", [P, 1])
        small = sb("small", [P, 320])
        work = sb("work", [P, 8560])

        def part(at, n, rows=P):
            return work[0:rows, at:at + n]

        shifted = part(0, 3 * 2 * 258).rearrange("p (r c t) -> p r c t", r=3, c=2)
        conv = part(1548, 3 * 2 * T).rearrange("p (r c t) -> p r c t", r=3, c=2)
        squares = part(3084, 1024).rearrange("p (b n) -> p b n", b=2)
        deviation = part(4108, T)
        hot_sb = part(4400, 512, BUCKETS + 1)
        table_sb = part(5424, HEADS, BUCKETS + 1)
        rows_sb = part(5440, 384, HEADS)
        rstd2 = part(5840, T)
        tokens = part(0, 2048).rearrange("p (j g t) -> p j g t", j=2, g=GROUPS)
        block_in = part(2048, 16 * 4 * NC)
        gelu = part(3008, 5 * 120).rearrange("p (k n) -> p k n", k=5)
        NS = 800
        soft = part(0, 3 * NS).rearrange("p (r n) -> p r n", r=3)
        probsT = part(3 * NS, 2 * 1024).rearrange("p (r n) -> p r n", r=2)
        Q0 = 3 * NS + 2048
        qT = part(Q0, 8 * T).rearrange("p (i t) -> p i t", i=8)
        keysT = part(Q0 + 2048, 4 * T).rearrange("p (i t) -> p i t", i=4)
        vals = part(Q0 + 3072, 2 * 512).rearrange("p (k n) -> p k n", k=2)
        assert Q0 + 4096 <= 8560
        kcT = small[:, 0:30].rearrange("p (a c) -> p a c", a=2)
        vc = small[0:NC, 32:288]
        stats = sb("stats", [P, 3, 24])
        gate = sb("gate", [P, 2, 3 * HEADS])
        rowmask = sb("rowmask", [P, 1])
        rstd_t = sb("rstd_t", [P, 4])

        bank = [ctx.enter_context(nc.psum_tensor(f"bank{i}", [P, 512], F32)) for i in range(8)]

        landed = [sem(f"landed{s}") for s in range(UP_SLOTS + 1)]
        x_landed, par_landed, hot_landed, bias_landed = sem("x_landed"), sem("par_landed"), sem("hot_landed"), sem("bias_landed")
        hi_up, lo_up, used_up = sem("hi_up"), sem("lo_up"), sem("used_up")
        hi_down, lo_down, used_down = sem("hi_down"), sem("lo_down"), sem("used_down")
        scaled, tapped, convolved, silued, y_done, y_hi_done, y_lo_done = (
            {s: sem(f"{n}_{s}") for s in ("a", "f0", "f1")}
            for n in ("scaled", "tapped", "convolved", "silued", "y_done", "y_hi_done", "y_lo_done"))
        acc_done, x_new = sem("acc_done"), sem("x_new")
        gx_hi_done, gx_lo_done = sem("gx_hi_done"), sem("gx_lo_done")
        gq_hi_done, gq_lo_done = sem("gq_hi_done"), sem("gq_lo_done")
        squared, summed, norm_summed = sem("squared"), sem("summed"), sem("norm_summed")
        deviated, rstd_done, padded = sem("deviated"), sem("rstd_done"), sem("padded")
        consts_done, table_done, rows_done, rows_copied = sem("consts_done"), sem("table_done"), sem("rows_done"), sem("rows_copied")
        rows_stored, bias_c_done, bias_c_copied = sem("rows_stored"), sem("bias_c_done"), sem("bias_c_copied")
        b_evacuated, tokens_shifted, block_done = sem("b_evacuated"), sem("tokens_shifted"), sem("block_done")
        block_hi_done, block_lo_done = sem("block_hi_done"), sem("block_lo_done")
        vals_done, gate_exp, gate_done, gate_step, gate_flipped = (
            sem("vals_done"), sem("gate_exp"), sem("gate_done"), sem("gate_step"), sem("gate_flipped"))
        pre_gelu, gelu_step, gelu_tanh, hidden_done = sem("pre_gelu"), sem("gelu_step"), sem("gelu_tanh"), sem("hidden_done")
        cmp_mm, cmp_done = sem("cmp_mm"), sem("cmp_done")
        scored, biased, maxed, exped = sem("scored"), sem("biased"), sem("maxed"), sem("exped")
        recipd, weighted, normed = sem("recipd"), sem("weighted"), sem("normed")
        turned0, turned1, probs0, probs1 = sem("turned0"), sem("turned1"), sem("probs0"), sem("probs1")
        headed, o_hi_done, o_lo_done = sem("headed"), sem("o_hi_done"), sem("o_lo_done")
        out_done, stored = sem("out_done"), sem("stored")

        NORM = {"a": 0, "f0": 1, "b": 2, "f1": 3, "end": 4}
        GAIN_OF = {"a": "mix0", "f0": "ffn0", "b": "kv", "f1": "ffn1"}
        LAST_DOWN = {n: piece[(st, "down", u, 0)]["n"] for n, st, u in (("f0", "a", AU - 1), ("b", "f0", FU - 1), ("f1", "o", 7), ("end", "f1", FU - 1))}
        RSTD_AT = {"a": 2, "f0": 3, "b": 5, "f1": 6, "end": 7}

        def looped(i):
            return not isinstance(i, int)

        ROUNDS = 6

        def gain(name, kt):
            at = PAR["gains"] + GAIN[name] * KT + kt
            return params[:, at:at + 1]

        def tap(st, c, i, k, ring, which):
            if st == "a":
                at = PAR["a_taps"] + 3 * k + which + 3 * ring * i
            else:
                at = PAR["f_taps"] + 3 * ((int(st[1]) * 2 + c) * FU + k) + which + 3 * ring * i
            return params[:, bass.ds(at, 1)]

        def piece_of(st, kind, k, c):
            return piece[(st, kind, k, c)]

        def stride(st, kind):
            return {"a": {"up": 6, "down": 2}}.get(st, {"up": 6, "down": 3})[kind]

        block = ctx.enter_context(nc.Block())

        @block.sync
        def _(sp):
            def load(st, kind, k, c, i=0):
                q = piece_of(st, kind, k, c)
                move = stride(st, kind) * i
                ring = 2 if st == "a" else 3
                s = min(q["slot"], UP_SLOTS)
                if kind == "up":
                    if q["prev"] is not None:
                        sp.wait_ge(lo_up, q["prev"] + 1 + move)
                elif q["n"] > 0:
                    sp.wait_ge(lo_down, q["n"] + move)
                unit = k + ring * i
                if st == "a":
                    src = a_up[unit, c] if kind == "up" else a_down[unit]
                elif st == "b":
                    src = b_up[k]
                elif st == "o":
                    src = b_down[k]
                else:
                    src = f_up[int(st[1]), unit, c] if kind == "up" else f_down[int(st[1]), unit]
                n = 8 * 3 * HEADS if st == "b" and B_ORDER[k][0] == "gate" else PW
                sp.dma_start(staged[:, s, 0:n], src[:, 0:n]).then_inc(landed[s], 16)

            def group(st, k, i=0):
                for c in range(3 if st == "a" else 2):
                    load(st, "up", k, c, i)
                load(st, "down", k, 0, i)

            for u in range(2):
                group("a", u)
            with sp.Fori(0, AU // 2 - 1) as i:
                for k in (2, 3):
                    group("a", k, i)
            for st in ("f0", "f1"):
                if st == "f0":
                    for u in range(3):
                        group(st, u)
                with sp.Fori(0, ROUNDS) as i:
                    for k in (3, 4, 5):
                        group(st, k, i)
                group(st, FU - 1)
                if st == "f0":
                    for b in range(NB):
                        load("b", "up", b, 0)
                    for i in range(3):
                        load("o", "down", i, 0)
                    for u in range(3):
                        for c in range(2):
                            load("f1", "up", u, c)
                    for i in range(3, 8):
                        load("o", "down", i, 0)
                    for u in range(3):
                        load("f1", "down", u, 0)
            for b in range(4):
                sp.wait_ge(out_done, 2 * b + 2)
                sp.dma_start(out[:, 2 * b:2 * b + 2, :], x[:, 2 * b:2 * b + 2, :]).then_inc(stored, 16)
            sp.wait_ge(stored, 64)

        @block.gpsimd
        def _(pool):
            nc.gpsimd.memset(ones[:], 1.0).then_inc(consts_done, 1)
            nc.gpsimd.memset(ident[:], 0.0).then_inc(consts_done, 1)
            nc.gpsimd.memset(eps[:], EPS).then_inc(consts_done, 1)
            nc.gpsimd.memset(rowmask[:], 1.0).then_inc(consts_done, 1)
            nc.gpsimd.memset(flip[:], 0.0).then_inc(consts_done, 1)
            pool.wait_ge(consts_done, 5)
            nc.gpsimd.affine_select(out=flip[:], in_=flip[:], compare_op=ALU.not_equal, fill=1.0, base=-(P - 1),
                                    pattern=[[1, P]], channel_multiplier=1).then_inc(consts_done, 1)
            nc.gpsimd.affine_select(out=ident[:], in_=ident[:], compare_op=ALU.not_equal, fill=1.0, base=0,
                                    pattern=[[-1, P]], channel_multiplier=1).then_inc(consts_done, 1)
            nc.gpsimd.affine_select(out=rowmask[:], in_=rowmask[:], compare_op=ALU.is_ge, fill=0.0, base=-(CL - 1),
                                    pattern=[[0, 1]], channel_multiplier=1).then_inc(consts_done, 1)

            def norm(st):
                k = NORM[st]
                for b in range(1, 4):
                    pool.wait_ge(squared, 4 * k + b + 1)
                    if b > 1:
                        pool.wait_ge(summed, 3 * k + b - 1)
                    nc.gpsimd.tensor_tensor(sumsq[:].rearrange("p h t -> p (h t)"), sumsq[:].rearrange("p h t -> p (h t)"),
                                            squares[:, b % 2, :], ALU.add).then_inc(summed, 1)

            def pads(n):
                nc.gpsimd.memset(shifted[:, :, :, 0:2], 0.0).then_inc(padded, 1)

            pads(0)
            norm("a")
            pool.wait_ge(rows_copied, 1)
            pool.dma_start(scratch, rows_sb).then_inc(rows_stored, 16)
            pool.wait_ge(rows_stored, 16)
            diagonals = bass.AP(tensor=scratch.tensor, offset=0, ap=[[1, P], [384, HEADS], [1, T]])
            pool.dma_start(bias[:], diagonals).then_inc(bias_landed, 16)
            norm("f0")
            norm("b")
            for e in range(HEADS):
                pool.wait_ge(weighted, e + 1)
                for n, (at, w) in enumerate(SPANS):
                    q = nc.gpsimd.tensor_scalar(soft[:, e % 3, at:at + w], soft[:, e % 3, at:at + w],
                                                stats[:, e % 3, 18 + n:19 + n], None, ALU.mult)
                q.then_inc(normed, 1)
            pool.wait_ge(headed, HEADS)
            pads(1)
            norm("f1")
            norm("end")

        @block.scalar
        def _(act):
            act.dma_start(x[:], xT).then_inc(x_landed, 16)
            act.dma_start(params[:], par).then_inc(par_landed, 16)
            act.dma_start(hot_sb, hot).then_inc(hot_landed, 16)
            act.dma_start(table_sb[0:BUCKETS, :], rel).then_inc(hot_landed, 16)

            def lead(st, kind, k, c, i=0):
                q = piece_of(st, kind, k, c)
                move = stride(st, kind) * i
                s = min(q["slot"], UP_SLOTS)
                hi, used = (hi_up, used_up) if kind == "up" else (hi_down, used_down)
                if kind == "up":
                    act.wait_ge(landed[s], 16 * q["turn"] + 16 * i)
                else:
                    act.wait_ge(landed[s], 16 * (q["n"] + 1) + 16 * move)
                if q["prev"] is not None:
                    act.wait_ge(used, q["prev"] + 1 + move)
                n = 8 * 3 * HEADS if st == "b" and B_ORDER[k][0] == "gate" else PW
                nc.scalar.activation(w_hi[:, q["slot"], 0:n], staged[:, s, 0:n], ACT.Copy).then_inc(hi, 1)

            def norm(st, first=False):
                k = NORM[st]
                for b in range(4):
                    act.wait_ge(x_landed, 16) if first else act.wait_ge(x_new, 4 * (k - 1) + b + 1)
                    if first and b == 0:
                        act.wait_ge(par_landed, 16)
                    if st != "end":
                        for kt in (2 * b, 2 * b + 1):
                            nc.scalar.activation(gx_hi[:, kt, :], x[:, kt, :], ACT.Copy,
                                                 scale=gain(GAIN_OF[st], kt)).then_inc(gx_hi_done, 1)
                    if b == 3:
                        act.wait_ge(summed, 3 * k + 1)
                    dst = sumsq[:].rearrange("p h t -> p (h t)") if b == 0 else squares[:, b % 2, :]
                    nc.scalar.activation(dst, x[:, 2 * b:2 * b + 2, :].rearrange("p k t -> p (k t)"),
                                         ACT.Square).then_inc(squared, 1)
                act.wait_ge(norm_summed, k + 1)
                q = nc.scalar.activation(deviation, bank[3][:, 0:T], ACT.Sqrt, bias=eps[:], scale=1.0 / D)
                if st == "b":
                    q = nc.scalar.activation(rstd_t[:, 2:4], bank[3][:, T:T + 2], ACT.Sqrt, bias=eps[:], scale=1.0 / D)
                q.then_inc(deviated, 1)

            def step(st, k, ahead, i=0):
                ring = 2 if st == "a" else 3
                r = k % ring
                u = k + ring * i
                if ahead:
                    lead(*ahead[0])
                for c in range(1 if st == "a" else 2):
                    if c == 0:
                        act.wait_ge(scaled[st], u + 1)
                    nc.scalar.activation(conv[:, r, c, :], shifted[:, r, c, 2:2 + T], ACT.Copy,
                                         scale=tap(st, c, i, k, ring, 2)).then_inc(tapped[st], 1)
                for q in ahead[1:-1]:
                    lead(*q)
                if st != "a":
                    act.wait_ge(convolved[st], 4 * u + 3)
                    nc.scalar.activation(conv[:, r, 0, :], conv[:, r, 0, :], ACT.Silu).then_inc(silued[st], 1)
                act.wait_ge(y_done[st], u + 1)
                q = piece_of(st, "down", k, 0)
                before = {"a": 2, "f0": 3, "f1": 3}[st]
                if k >= before or looped(i):
                    act.wait_ge(used_down, q["n"] - before + 1 + stride(st, "down") * i)
                nc.scalar.activation(y_hi[:, r * T:(r + 1) * T], conv[:, r, 1, :], ACT.Copy).then_inc(y_hi_done[st], 1)
                if ahead:
                    lead(*ahead[-1])

            def stage(st, nxt):
                if st == "a":
                    step(st, 0, group("a", 2))
                    step(st, 1, group("a", 3))
                    with act.Fori(0, 2) as i:
                        for k in (2, 3):
                            step(st, k, group("a", k + 2, i), i)
                    step(st, 6, nxt[0])
                    step(st, 7, nxt[1])
                else:
                    step(st, 0, group(st, 2))
                    with act.Fori(0, ROUNDS) as i:
                        for k in (1, 2, 3):
                            step(st, k, group(st, k + 2, i), i)
                    step(st, 19, group(st, 21))
                    step(st, 20, nxt[0])
                    step(st, 21, nxt[1])

            for u in range(2):
                for q in group("a", u):
                    lead(*q)
                if u == 0:
                    norm("a", first=True)
            stage("a", [group("f0", 0), group("f0", 1)])
            norm("f0")
            stage("f0", [[("b", "up", 0, 0), ("b", "up", 1, 0)], [("b", "up", 2, 0), ("b", "up", 3, 0)]])
            norm("b")
            for kt in range(KT):
                nc.scalar.activation(gq_hi[:, kt, :], x[:, kt, :], ACT.Copy, scale=gain("mix1", kt)).then_inc(gq_hi_done, 1)
            lead("b", "up", 4, 0)
            lead("b", "up", 5, 0)

            UB = piece[("b", "up", 0, 0)]["n"]
            for b, (what, t) in enumerate(B_ORDER):
                if b in (2, 4):
                    j = b // 2 - 1
                    act.wait_ge(b_evacuated, 2 * j + 2)
                    nc.scalar.activation(tokens[HD:P, j, :, 0:T - 1], tokens[0:HD, j, :, 1:T], ACT.Copy).then_inc(tokens_shifted, 1)
                if b in (6, 14):
                    j = 0 if b == 6 else 1
                    act.wait_ge(block_done, j + 1)
                    if j:
                        act.wait_ge(used_up, UB + B_ORDER.index(("w1", 1)) + 1)
                    nc.scalar.activation(y_hi[:], block_in, ACT.Copy).then_inc(block_hi_done, 1)
                if what == "val" and t == 3:
                    act.wait_ge(used_up, UB + b + 1)
                    act.wait_ge(rstd_done, RSTD_AT["b"])
                    for k in range(2):
                        nc.scalar.activation(vals[:, k, :], bank[4 + k][:], ACT.Copy, scale=rstd_t[:, k:k + 1]).then_inc(vals_done, 1)
                if what == "gate":
                    act.wait_ge(gate_step, 1)
                    act.wait_ge(used_up, UB + b + 1)
                    for k in range(2):
                        q = nc.scalar.activation(gate[:, k, :], bank[7][:, 64 * k:64 * k + 3 * HEADS], ACT.Exp,
                                                 scale=rstd_t[:, 2 + k:3 + k])
                    q.then_inc(gate_exp, 1)
                if what == "w1" and t in (1, 3):
                    j = t // 2
                    act.wait_ge(used_up, UB + b + 1)
                    nc.scalar.activation(gelu[:, 0, 60 * j:60 * j + 60], bank[6][:, 60 * j:60 * j + 60], ACT.Identity,
                                         bias=params[:, PAR["b1"] + j:PAR["b1"] + j + 1]).then_inc(pre_gelu, 1)
                if b + 6 < NB:
                    lead("b", "up", b + 6, 0)
            act.wait_ge(gelu_step, 3)
            nc.scalar.activation(gelu[:, 3, :], gelu[:, 2, :], ACT.Tanh, scale=math.sqrt(2 / math.pi)).then_inc(gelu_tanh, 1)

            later = [("o", "down", 0, 0), ("o", "down", 1, 0), ("o", "down", 2, 0)] + [
                ("f1", "up", u, c) for u in range(2) for c in range(2)]
            for e in range(HEADS + 3):
                if e < HEADS:
                    act.wait_ge(maxed, e + 1)
                    if e >= 3:
                        act.wait_ge(recipd, e - 2)
                    for n, (at, w) in enumerate(SPANS):
                        q = nc.scalar.activation(soft[:, e % 3, at:at + w], soft[:, e % 3, at:at + w], ACT.Exp,
                                                 bias=stats[:, e % 3, 6 + n:7 + n], accum_out=stats[:, e % 3, 12 + n:13 + n])
                    q.then_inc(exped, 1)
                if 2 <= e < HEADS + 2:
                    h = e - 2
                    act.wait_ge(turned0, h + 1)
                    if h >= 2:
                        act.wait_ge(headed, h - 1)
                    nc.scalar.activation(probsT[:, h % 2, 0:512], bank[4][:], ACT.Copy).then_inc(probs0, 1)
                if e >= 3 and (e - 3) % 2 == 1:
                    i = (e - 3) // 2
                    act.wait_ge(headed, 2 * i + 2)
                    nc.scalar.activation(gx_hi[:, i, :].rearrange("p (k t) -> p k t", k=2), backwards(bank[6 + i % 2][:, 0:T]),
                                         ACT.Copy).then_inc(o_hi_done, 1)
                if e % 2 == 1 and e // 2 < len(later):
                    lead(*later[e // 2])
            for i in range(3, 8):
                lead("o", "down", i, 0)
            lead("f1", "down", 0, 0)
            norm("f1")
            lead("f1", "down", 1, 0)
            stage("f1", [[], []])
            norm("end")

        @block.vector
        def _(dve):
            def rest(st, kind, k, c, i=0):
                q = piece_of(st, kind, k, c)
                move = stride(st, kind) * i
                s = min(q["slot"], UP_SLOTS)
                hi, lo = (hi_up, lo_up) if kind == "up" else (hi_down, lo_down)
                dve.wait_ge(hi, q["n"] + 1 + move)
                n = 8 * 3 * HEADS if st == "b" and B_ORDER[k][0] == "gate" else PW
                nc.vector.tensor_tensor(w_lo[:, q["slot"], 0:n], staged[:, s, 0:n], w_hi[:, q["slot"], 0:n].bitcast(F32),
                                        ALU.subtract).then_inc(lo, 1)

            def norm(st, first=False):
                k = NORM[st]
                for b in range(4):
                    if not first:
                        if b < 3:
                            dve.wait_ge(acc_done, 3 * (k - 1) + b + 1)
                        else:
                            dve.wait_ge(used_down, LAST_DOWN[st] + 1)
                        xb = x[:, 2 * b:2 * b + 2, :].rearrange("p k t -> p (k t)")
                        nc.vector.tensor_tensor(xb, xb, bank[4 + b][:], ALU.add).then_inc(x_new, 1)
                    if st != "end":
                        for kt in (2 * b, 2 * b + 1):
                            dve.wait_ge(gx_hi_done, 8 * k + kt + 1)
                            if first and kt == 0:
                                dve.wait_ge(par_landed, 16)
                                dve.wait_ge(x_landed, 16)
                            nc.vector.scalar_tensor_tensor(gx_lo[:, kt, :], x[:, kt, :], gain(GAIN_OF[st], kt),
                                                           gx_hi[:, kt, :].bitcast(F32), ALU.mult, ALU.subtract).then_inc(gx_lo_done, 1)
                dve.wait_ge(deviated, k + 1)
                nc.vector.reciprocal(rstd[:], deviation).then_inc(rstd_done, 1)
                if st == "a":
                    dve.wait_ge(rstd_done, 1)
                    nc.vector.tensor_tensor(rstd2, rstd[:], rstd[:], ALU.mult).then_inc(rstd_done, 1)
                elif st == "b":
                    nc.vector.reciprocal(rstd_t[:, 0:2], rstd_t[:, 2:4]).then_inc(rstd_done, 1)
                dve.wait_ge(rstd_done, RSTD_AT[st])

            def step(st, k, ahead, i=0):
                ring = 2 if st == "a" else 3
                r = k % ring
                u = k + ring * i
                last = piece_of(st, "up", k, 2 if st == "a" else 1)
                dve.wait_ge(used_up, last["n"] + 1 + stride(st, "up") * i)
                if st == "a":
                    nc.vector.tensor_tensor(shifted[:, r, 1, 2:2 + T], bank[2 * r][:, 0:T], rstd[:], ALU.mult)
                    nc.vector.tensor_tensor(conv[:, r, 1, :], bank[2 * r][:, T:2 * T], rstd2, ALU.mult).then_inc(convolved[st], 1)
                    dve.wait_ge(convolved[st], 3 * u + 1)
                    nc.vector.tensor_tensor(shifted[:, r, 0, 2:2 + T], bank[2 * r + 1][:, 0:T], conv[:, r, 1, :],
                                            ALU.mult).then_inc(scaled[st], 1)
                    halves, per, off = 1, 3, 1
                else:
                    nc.vector.tensor_tensor(shifted[:, r, :, 2:2 + T], bank[r][:].rearrange("p (c t) -> p c t", c=2),
                                            rstd[:].unsqueeze(1).to_broadcast([P, 2, T]), ALU.mult).then_inc(scaled[st], 1)
                    halves, per, off = 2, 4, 0
                if ahead:
                    rest(*ahead[0])
                for c in range(halves):
                    dve.wait_ge(tapped[st], halves * u + c + 1)
                    nc.vector.scalar_tensor_tensor(conv[:, r, c, :], shifted[:, r, c, 1:1 + T], tap(st, c, i, k, ring, 1),
                                                   conv[:, r, c, :], ALU.mult, ALU.add).then_inc(convolved[st], 1)
                for c in range(halves):
                    dve.wait_ge(convolved[st], per * u + off + c + 1)
                    nc.vector.scalar_tensor_tensor(conv[:, r, c, :], shifted[:, r, c, 0:T], tap(st, c, i, k, ring, 0),
                                                   conv[:, r, c, :], ALU.mult, ALU.add).then_inc(convolved[st], 1)
                for q in ahead[1:-1]:
                    rest(*q)
                dve.wait_ge(convolved[st], per * u + per)
                if st == "a":
                    nc.vector.tensor_tensor(conv[:, r, 1, :], conv[:, r, 0, :], shifted[:, r, 1, 2:2 + T],
                                            ALU.mult).then_inc(y_done[st], 1)
                else:
                    dve.wait_ge(silued[st], u + 1)
                    nc.vector.tensor_tensor(conv[:, r, 1, :], conv[:, r, 0, :], conv[:, r, 1, :],
                                            ALU.mult).then_inc(y_done[st], 1)
                dve.wait_ge(y_hi_done[st], u + 1)
                nc.vector.tensor_tensor(y_lo[:, r * T:(r + 1) * T], conv[:, r, 1, :], y_hi[:, r * T:(r + 1) * T].bitcast(F32),
                                        ALU.subtract).then_inc(y_lo_done[st], 1)
                if ahead:
                    rest(*ahead[-1])

            def stage(st, nxt):
                if st == "a":
                    step(st, 0, group("a", 2))
                    step(st, 1, group("a", 3))
                    with dve.Fori(0, 2) as i:
                        for k in (2, 3):
                            step(st, k, group("a", k + 2, i), i)
                    step(st, 6, nxt[0])
                    step(st, 7, nxt[1])
                else:
                    step(st, 0, group(st, 2))
                    with dve.Fori(0, ROUNDS) as i:
                        for k in (1, 2, 3):
                            step(st, k, group(st, k + 2, i), i)
                    step(st, 19, group(st, 21))
                    step(st, 20, nxt[0])
                    step(st, 21, nxt[1])

            nc.vector.memset(table_sb[BUCKETS:BUCKETS + 1, :], NEG).then_inc(table_done, 1)
            dve.wait_ge(rows_done, 1)
            nc.vector.tensor_copy(rows_sb, bank[4][0:HEADS, 0:384]).then_inc(rows_copied, 1)
            dve.wait_ge(bias_c_done, 1)
            nc.vector.tensor_copy(bias_c[:].rearrange("p k h c -> p k c h"),
                                  bank[5][:, 0:2 * NC * HEADS].rearrange("p (k c h) -> p k c h", k=2, c=NC)).then_inc(bias_c_copied, 1)

            for u in range(2):
                for q in group("a", u):
                    rest(*q)
                if u == 0:
                    norm("a", first=True)
            dve.wait_ge(padded, 1)
            stage("a", [group("f0", 0), group("f0", 1)])
            norm("f0")
            stage("f0", [[("b", "up", 0, 0), ("b", "up", 1, 0)], [("b", "up", 2, 0), ("b", "up", 3, 0)]])
            norm("b")
            nc.vector.tensor_scalar(rstd_t[:, 2:4], rstd_t[:, 0:2], -1.0, None, ALU.mult).then_inc(gate_step, 1)
            for kt in range(KT):
                dve.wait_ge(gq_hi_done, kt + 1)
                nc.vector.scalar_tensor_tensor(gq_lo[:, kt, :], x[:, kt, :], gain("mix1", kt), gq_hi[:, kt, :].bitcast(F32),
                                               ALU.mult, ALU.subtract).then_inc(gq_lo_done, 1)
            rest("b", "up", 4, 0)
            rest("b", "up", 5, 0)

            UB = piece[("b", "up", 0, 0)]["n"]
            steps = 0
            for b, (what, t) in enumerate(B_ORDER):
                if what in ("cmp", "key", "q"):
                    dve.wait_ge(used_up, UB + b + 1)
                    e = b if b < 8 else 8 + t
                    src = bank[e % 3][:, 0:T]
                if what == "cmp":
                    j, a = t // 2, t % 2
                    for p in range(2):
                        q = nc.vector.tensor_tensor(tokens[0:HD, j, 2 * a + p, :], src[HD * p:HD * p + HD, :],
                                                    rstd[0:HD, :], ALU.mult)
                    q.then_inc(b_evacuated, 1)
                elif what == "key":
                    nc.vector.tensor_tensor(keysT[:, t, :], src, rstd[:], ALU.mult).then_inc(b_evacuated, 1)
                elif what == "q":
                    nc.vector.scalar_tensor_tensor(backwards(qT[:, t, :]), src.rearrange("p (k t) -> p k t", k=2), HD ** -0.5,
                                                   rstd[:].rearrange("p (k t) -> p k t", k=2), ALU.mult, ALU.mult).then_inc(b_evacuated, 1)
                if b in (4, 10):
                    j = 0 if b == 4 else 1
                    dve.wait_ge(tokens_shifted, j + 1)
                    if j:
                        dve.wait_ge(block_lo_done, 1)
                    tok, pe_j = tokens[:, j, 0, 0:1], params[:, PAR["pe"] + 16 * j:PAR["pe"] + 16 * j + 16]
                    tok = bass.AP(tensor=tok.tensor, offset=tok.offset, ap=[tok.ap[0], [2, 16], [T, GROUPS], [CS, NC]])
                    pe_j = pe_j.unsqueeze(2).unsqueeze(3).to_broadcast([P, 16, GROUPS, NC])
                    q = nc.vector.tensor_tensor(block_in.rearrange("p (i g c) -> p i g c", i=16, g=GROUPS), tok, pe_j, ALU.add)
                    q.then_inc(block_done, 1)
                if b in (6, 16):
                    j = 0 if b == 6 else 1
                    dve.wait_ge(block_hi_done, j + 1)
                    nc.vector.tensor_tensor(y_lo[:], block_in, y_hi[:].bitcast(F32), ALU.subtract).then_inc(block_lo_done, 1)
                if b == 18:
                    dve.wait_ge(gate_exp, 1)
                    dve.wait_ge(consts_done, 8)
                    nc.vector.tensor_scalar(gate[:], gate[:], 1.0, None, ALU.add).then_inc(gate_step, 1)
                    dve.wait_ge(gate_step, 2)
                    nc.vector.reciprocal(gate[:], gate[:]).then_inc(gate_step, 1)
                    dve.wait_ge(gate_step, 3)
                    first = gate[:, 0, 0:3 * HEADS:3]
                    nc.vector.tensor_scalar(first, first, rowmask[:], None, ALU.mult).then_inc(gate_done, 1)
                if b == 20:
                    dve.wait_ge(gate_flipped, 1)
                    nc.vector.tensor_copy(gate[:].rearrange("p k n -> p (k n)"), bank[7][:, 128:128 + 6 * HEADS]).then_inc(gate_done, 1)
                if b == 21:
                    dve.wait_ge(pre_gelu, 2)
                    z, a1, a2, th, hid = (gelu[:, n, :] for n in range(5))
                    nc.vector.tensor_tensor(a1, z, z, ALU.mult).then_inc(gelu_step, 1)
                    dve.wait_ge(gelu_step, 1)
                    nc.vector.tensor_scalar(a1, a1, 0.044715, 1.0, ALU.mult, ALU.add).then_inc(gelu_step, 1)
                    dve.wait_ge(gelu_step, 2)
                    nc.vector.tensor_tensor(a2, a1, z, ALU.mult).then_inc(gelu_step, 1)
                if b + 6 < NB:
                    rest("b", "up", b + 6, 0)
            dve.wait_ge(gelu_tanh, 1)
            nc.vector.tensor_scalar(th, th, 1.0, 0.5, ALU.add, ALU.mult).then_inc(gelu_step, 1)
            dve.wait_ge(gelu_step, 4)
            nc.vector.tensor_tensor(hid, th, z, ALU.mult).then_inc(hidden_done, 1)
            dve.wait_ge(cmp_mm, 1)
            for p in range(2):
                nc.vector.tensor_copy(kcT[HD * p:HD * p + HD, :, :],
                                      bank[6][0:HD, 128:128 + 60].rearrange("p (a q c) -> p a q c", a=2, q=2)[:, :, p, :])
            nc.vector.tensor_copy(vc, bank[6][0:NC, 256:512]).then_inc(cmp_done, 1)
            dve.wait_ge(bias_landed, 16)
            dve.wait_ge(bias_c_copied, 1)
            dve.wait_ge(gate_done, 2)

            later = [("o", "down", 0, 0), ("o", "down", 1, 0), ("o", "down", 2, 0)] + [
                ("f1", "up", u, c) for u in range(2) for c in range(2)]
            for e in range(HEADS + 3):
                if e < HEADS:
                    h = head_of(e)
                    r = e % 3
                    dve.wait_ge(scored, e + 1)
                    if e >= 3:
                        dve.wait_ge(turned1, e - 2)
                    s0, s1 = bank[2 * (e % 2)], bank[2 * (e % 2) + 1]
                    near = bias[:, h, P:T]
                    srcs = [(s0[:, 2 * P:2 * P + NC], bias_c[:, 0, h, :]), (s0[:, 0:P], near), (s0[:, P:2 * P], near),
                            (s0[:, 2 * P + NC:2 * P + 2 * NC], bias_c[:, 1, h, :]), (s1[:, 0:T], bias[:, h, :]), (s1[:, T:2 * T], bias[:, h, :])]
                    for n, ((at, w), (sc, bi)) in enumerate(zip(SPANS, srcs)):
                        q = nc.vector.tensor_tensor_reduce(soft[:, r, at:at + w], sc, bi, 1.0, -3.0e38, ALU.add, ALU.max,
                                                           stats[:, r, n:n + 1])
                    q.then_inc(biased, 1)
                    dve.wait_ge(biased, e + 1)
                    nc.vector.tensor_scalar(stats[:, r, 6:12], stats[:, r, 0:6], -1.0, None, ALU.mult).then_inc(maxed, 1)
                if 1 <= e < HEADS + 1:
                    g, r = e - 1, (e - 1) % 3
                    h = head_of(g)
                    dve.wait_ge(exped, g + 1)
                    nc.vector.reciprocal(stats[:, r, 18:24], stats[:, r, 12:18]).then_inc(recipd, 1)
                    dve.wait_ge(recipd, g + 1)
                    w = stats[:, r, 18:24].rearrange("p (k b) -> p k b", k=2)
                    nc.vector.tensor_tensor(w, w, gate[:, :, 3 * h:3 * h + 3], ALU.mult).then_inc(weighted, 1)
                if 2 <= e < HEADS + 2:
                    g = e - 2
                    dve.wait_ge(turned1, g + 1)
                    if g >= 2:
                        dve.wait_ge(headed, g - 1)
                    nc.vector.tensor_copy(probsT[:, g % 2, 512:768], bank[5][:, 0:T])
                    nc.vector.tensor_copy(probsT[0:NC, g % 2, 768:1024], bank[5][0:NC, T:2 * T]).then_inc(probs1, 1)
                if e >= 3 and (e - 3) % 2 == 1:
                    i = (e - 3) // 2
                    dve.wait_ge(o_hi_done, i + 1)
                    nc.vector.tensor_tensor(gx_lo[:, i, :].rearrange("p (k t) -> p k t", k=2), backwards(bank[6 + i % 2][:, 0:T]),
                                            gx_hi[:, i, :].bitcast(F32).rearrange("p (k t) -> p k t", k=2),
                                            ALU.subtract).then_inc(o_lo_done, 1)
                if e % 2 == 1 and e // 2 < len(later):
                    rest(*later[e // 2])
            for i in range(3, 8):
                rest("o", "down", i, 0)
            rest("f1", "down", 0, 0)
            norm("f1")
            dve.wait_ge(padded, 2)
            rest("f1", "down", 1, 0)
            stage("f1", [[], []])
            norm("end")
            for kt in range(KT):
                nc.vector.scalar_tensor_tensor(x[:, kt, :], x[:, kt, :], gain("final", kt), rstd[:], ALU.mult,
                                               ALU.mult).then_inc(out_done, 1)

        @block.tensor
        def _(pe):
            def three(out_ap, whi, wlo, xhi, xlo, start, stop):
                nc.tensor.matmul(out_ap, whi, xhi, start=start, stop=False, skip_group_check=True)
                nc.tensor.matmul(out_ap, whi, xlo, start=False, stop=False, skip_group_check=True)
                return nc.tensor.matmul(out_ap, wlo, xhi, start=False, stop=stop, skip_group_check=True)

            def product(q, dst, xh, xl, first, move=0, fresh=None, hi_sem=None):
                s = q["slot"]
                pe.wait_ge(lo_up, q["n"] + 1 + move)
                for kt in range(KT):
                    if fresh is not None:
                        pe.wait_ge(fresh, hi_sem + kt + 1)
                    mm = three(dst, w_hi[:, s, kt * P:kt * P + P], w_lo[:, s, kt * P:kt * P + P],
                               xh[:, kt, :], xl[:, kt, :], first and kt == 0, kt == KT - 1)
                mm.then_inc(used_up, 1)

            def up(st, k, i=0):
                fresh = (gx_lo_done, 8 * NORM[st]) if k == 0 else (None, None)
                ring = 2 if st == "a" else 3
                if k >= ring:
                    pe.wait_ge(scaled[st], k - ring + 1 + ring * i)
                move = stride(st, "up") * i
                for c in range(3 if st == "a" else 2):
                    q = piece_of(st, "up", k, c)
                    if st == "a":
                        b, half = 2 * (k % 2) + c // 2, c % 2
                    else:
                        b, half = k % 3, c
                    product(q, bank[b][:, half * T:(half + 1) * T], gx_hi, gx_lo, half == 0, move, *fresh)

            def down(st, k, units, i=0, yh=None, yl=None, ready=None, at=None):
                r = k % (2 if st == "a" else 3)
                q = piece_of(st, "down", k, 0)
                if ready is None:
                    pe.wait_ge(y_lo_done[st], k + 1 + (2 if st == "a" else 3) * i)
                    yh, yl = y_hi[:, r * T:(r + 1) * T], y_lo[:, r * T:(r + 1) * T]
                else:
                    pe.wait_ge(ready, at)
                pe.wait_ge(lo_down, q["n"] + 1 + stride(st, "down") * i)
                s = q["slot"]
                first, last = (not looped(i) and k == 0), (not looped(i) and k == units - 1)
                for m in range(KT):
                    mm = three(bank[4 + m // 2][:, (m % 2) * T:(m % 2 + 1) * T], w_hi[:, s, m * P:m * P + P],
                               w_lo[:, s, m * P:m * P + P], yh, yl, first and m % 2 == 0, last)
                    if last and m in (1, 3, 5):
                        mm.then_inc(acc_done, 1)
                mm.then_inc(used_down, 1)

            def norm(st):
                k = NORM[st]
                pe.wait_ge(summed, 3 * k + 3)
                if k == 0:
                    pe.wait_ge(consts_done, 8)
                for h in range(2):
                    mm = nc.tensor.matmul(bank[3][:, 0:T], ones[:], sumsq[:, h, :], start=h == 0, stop=h == 1, skip_group_check=True)
                if st == "b":
                    for t in range(2):
                        for h in range(2):
                            mm = nc.tensor.matmul(bank[3][:, T + t:T + t + 1], sumsq[:, h, t * P:t * P + P], ones[:, 0:1],
                                                  start=False, stop=h == 1, skip_group_check=True)
                mm.then_inc(norm_summed, 1)

            def stage(st):
                up(st, 0)
                norm(st)
                if st == "a":
                    pe.wait_ge(deviated, 1)
                    up(st, 1)
                    down(st, 0, AU)
                    with pe.Fori(0, AU // 2 - 1) as i:
                        for k in (2, 3):
                            unit(st, k, i)
                    down(st, AU - 1, AU)
                else:
                    up(st, 1)
                    down(st, 0, FU)
                    up(st, 2)
                    down(st, 1, FU)
                    with pe.Fori(0, ROUNDS) as i:
                        for k in (3, 4, 5):
                            unit(st, k, i)
                    unit(st, 21)
                    down(st, 21, FU)

            def unit(st, k, i=0):
                up(st, k, i)
                down(st, k - 1, AU if st == "a" else FU, i)

            pe.wait_ge(hot_landed, 32)
            pe.wait_ge(table_done, 1)
            nc.tensor.matmul(bank[4][0:HEADS, 0:384], table_sb, hot_sb[:, 0:384], start=True, stop=True).then_inc(rows_done, 1)
            for k in range(2):
                for c in range(NC):
                    at = 255 - (P * k + P - 1 - CS * c - (CL - 1))
                    j = (k * NC + c) * HEADS
                    mm = nc.tensor.matmul(bank[5][:, j:j + HEADS], hot_sb[:, at:at + P], table_sb, start=True, stop=True)
            mm.then_inc(bias_c_done, 1)

            stage("a")
            stage("f0")

            UB = piece[("b", "up", 0, 0)]["n"]
            for b, (what, t) in enumerate(B_ORDER):
                q = piece_of("b", "up", b, 0)
                s = q["slot"]
                if what in ("cmp", "key", "q"):
                    e = b if b < 8 else 8 + t
                    if e >= 3:
                        pe.wait_ge(b_evacuated, e - 2)
                    if what == "q":
                        product(q, bank[e % 3][:, 0:T], gq_hi, gq_lo, True, 0, gq_lo_done if t == 0 else None, 0)
                    else:
                        product(q, bank[e % 3][:, 0:T], gx_hi, gx_lo, True, 0, gx_lo_done if b == 0 else None, 8 * NORM["b"])
                    if b == 1:
                        norm("b")
                    if b == 20:
                        pe.wait_ge(gate_done, 1)
                        nc.tensor.matmul(bank[7][:, 128:128 + 6 * HEADS], flip[:], gate[:].rearrange("p k n -> p (k n)"),
                                         start=True, stop=True).then_inc(gate_flipped, 1)
                    continue
                pe.wait_ge(lo_up, q["n"] + 1)
                if what == "val":
                    if t == 0:
                        pe.wait_ge(x_new, 8)
                    for tt in range(2):
                        for kk in range(2):
                            kt = 2 * t + kk
                            mm = three(bank[4 + tt][:], gx_hi[:, kt, tt * P:tt * P + P], gx_lo[:, kt, tt * P:tt * P + P],
                                       w_hi[:, s, kk * 512:kk * 512 + 512], w_lo[:, s, kk * 512:kk * 512 + 512],
                                       kt == 0, kt == KT - 1)
                elif what == "w1":
                    j = t // 2
                    if t % 2 == 0:
                        pe.wait_ge(block_lo_done, j + 1)
                    if t == 2:
                        pe.wait_ge(pre_gelu, 1)
                    for i8 in range(8):
                        i = 8 * (t % 2) + i8
                        mm = three(bank[6][:, 60 * j:60 * j + 60], w_hi[:, s, i8 * P:i8 * P + P], w_lo[:, s, i8 * P:i8 * P + P],
                                   y_hi[:, 60 * i:60 * i + 60], y_lo[:, 60 * i:60 * i + 60], i == 0, i == 15)
                elif what == "gate":
                    pe.wait_ge(gq_lo_done, 8)
                    for tt in range(2):
                        for kt in range(KT):
                            mm = three(bank[7][:, 64 * tt:64 * tt + 48], gq_hi[:, kt, tt * P:tt * P + P],
                                       gq_lo[:, kt, tt * P:tt * P + P], w_hi[:, s, 48 * kt:48 * kt + 48],
                                       w_lo[:, s, 48 * kt:48 * kt + 48], tt == 0 and kt == 0, kt == KT - 1)
                mm.then_inc(used_up, 1)

            pe.wait_ge(hidden_done, 1)
            hid = gelu[:, 4, :]
            w2 = params[:, PAR["w2"]:PAR["w2"] + 2 * HD]
            nc.tensor.matmul(bank[6][0:HD, 128:188], w2[:, 0:HD], hid[:, 0:60], start=True, stop=True)
            for g in range(GROUPS):
                mm = nc.tensor.matmul(bank[6][0:NC, 256 + HD * g:256 + HD * g + HD], hid[:, 60 + NC * g:60 + NC * g + NC],
                                      w2[:, HD:2 * HD], start=True, stop=True)
            mm.then_inc(cmp_mm, 1)

            pe.wait_ge(cmp_done, 1)
            pe.wait_ge(b_evacuated, 16)
            pe.wait_ge(vals_done, 2)
            for e in range(HEADS + 3):
                if e < HEADS:
                    i, p = e // 2, e % 2
                    a = i // 4
                    rows = slice(HD * p, HD * p + HD)
                    s0, s1 = bank[2 * p], bank[2 * p + 1]
                    if e >= 2:
                        pe.wait_ge(biased, e - 1)
                    for t in range(2):
                        lhs = qT[rows, i, t * P:t * P + P]
                        if t == 0:
                            nc.tensor.matmul(s0[:, 0:P], lhs, keysT[rows, a, 0:P], start=True, stop=True)
                            nc.tensor.matmul(s0[:, P:2 * P], lhs, keysT[rows, 2 + a, 0:P], start=True, stop=True)
                        else:
                            nc.tensor.matmul(s1[:, 0:T], lhs, keysT[rows, a, :], start=True, stop=True)
                            nc.tensor.matmul(s1[:, T:2 * T], lhs, keysT[rows, 2 + a, :], start=True, stop=True)
                        mm = nc.tensor.matmul(s0[:, 2 * P + NC * t:2 * P + NC * t + NC], lhs, kcT[rows, a, :], start=True, stop=True)
                    mm.then_inc(scored, 1)
                if 2 <= e < HEADS + 2:
                    g = e - 2
                    pe.wait_ge(normed, g + 1)
                    if g >= 1:
                        pe.wait_ge(probs0, g)
                    sp0 = [SPANS[1], SPANS[4], SPANS[2], SPANS[5]]
                    for n, (at, w) in enumerate(sp0):
                        mm = nc.tensor.transpose(bank[4][:, n * P:n * P + P], soft[:, g % 3, at:at + P], ident[:])
                    mm.then_inc(turned0, 1)
                    if g >= 1:
                        pe.wait_ge(probs1, g)
                    for n, (at, w) in enumerate([SPANS[4], SPANS[5]]):
                        nc.tensor.transpose(bank[5][:, n * P:n * P + P], soft[:, g % 3, at + P:at + T], ident[:])
                    for n, (at, w) in enumerate([SPANS[0], SPANS[3]]):
                        mm = nc.tensor.transpose(bank[5][0:NC, T + n * P:T + n * P + P], soft[:, g % 3, at:at + NC], ident[:])
                    mm.then_inc(turned1, 1)
                if e >= 3:
                    g = e - 3
                    i, p = g // 2, g % 2
                    grp = head_of(g) // HPG
                    pt = probsT[:, g % 2, :]
                    pe.wait_ge(probs0, g + 1)
                    pe.wait_ge(probs1, g + 1)
                    if p == 0 and i >= 2:
                        pe.wait_ge(o_lo_done, i - 1)
                    dst = bank[6 + i % 2][HD * p:HD * p + HD, 0:T]
                    slc, win = (vals[:, :, n * T + HD * grp:n * T + HD * grp + HD] for n in range(2))
                    nc.tensor.matmul(dst, slc[:, 0], pt[:, 0:T], start=True, stop=False, skip_group_check=True)
                    nc.tensor.matmul(dst, win[:, 0], pt[:, T:2 * T], start=False, stop=False, skip_group_check=True)
                    nc.tensor.matmul(dst[:, P:T], slc[:, 1], pt[:, 512:640], start=False, stop=False, skip_group_check=True)
                    nc.tensor.matmul(dst[:, P:T], win[:, 1], pt[:, 640:768], start=False, stop=False, skip_group_check=True)
                    mm = nc.tensor.matmul(dst, vc[:, HD * grp:HD * grp + HD], pt[0:NC, 768:1024], start=False, stop=True,
                                          skip_group_check=True)
                    mm.then_inc(headed, 1)
            for i in range(8):
                down("o", i, 8, 0, gx_hi[:, i, :], gx_lo[:, i, :], o_lo_done, 8)
            stage("f1")
            norm("end")


SPANS = [(0, NC), (16, P), (16 + P, P), (16 + 2 * P, NC), (32 + 2 * P, T), (32 + 2 * P + T, T)]


def head_of(e):
    i, p = e // 2, e % 2
    return (2 * (i // HPG) + p) * HPG + i % HPG


def backwards(ap):
    return ap.rearrange("p (k t) -> p k t", k=2)[:, :, ::-1]


def group(st, k, i=0):
    return [(st, "up", k, c, i) for c in range(3 if st == "a" else 2)] + [(st, "down", k, 0, i)]


def kernel(x, mix_norm, a_w_in, a_conv, a_w_out, ffn_norm, ffn_up, ffn_conv, ffn_down, kv_norm, w_kv, cmp_pe,
           cmp_w1, cmp_b1, cmp_w2, b_w_qg, b_w_o, rel_bias, final_norm):
    import concourse.bacc as bacc
    from concourse.bass_utils import run_bass_kernel_spmd as run

    c = lambda a: np.ascontiguousarray(np.asarray(a))
    tiles = lambda w, n: c(np.asarray(w).reshape(KT, P, n, P).transpose(2, 1, 0, 3)).reshape(n, P, PW)
    feat = lambda v: np.asarray(v).reshape(-1, P).T
    hd = HEADS * HD
    gains = np.concatenate([feat(v) for v in (mix_norm[0], ffn_norm[0], kv_norm, mix_norm[1], ffn_norm[1], final_norm)], 1)
    a_taps = np.asarray(a_conv)[0].reshape(3, AU, P).transpose(2, 1, 0).reshape(P, -1)
    f_taps = np.asarray(ffn_conv).reshape(2, 3, 2 * FU, P).transpose(3, 0, 2, 1).reshape(P, -1)
    pe = np.asarray(cmp_pe).reshape(2, 16, P).transpose(2, 0, 1).reshape(P, -1)
    w2 = np.asarray(cmp_w2).transpose(1, 0, 2).reshape(P, -1)
    par = np.concatenate([gains, a_taps, f_taps, pe, np.asarray(cmp_b1).T, w2], 1)
    a_up = tiles(np.asarray(a_w_in)[0], 3 * AU).reshape(3, AU, P, PW).transpose(1, 0, 2, 3)
    f_up = np.stack([tiles(w, 2 * FU).reshape(2, FU, P, PW).transpose(1, 0, 2, 3) for w in np.asarray(ffn_up)])
    kv = np.asarray(w_kv).reshape(D, 6, GROUPS * HD)
    kv_tiles = lambda s: list(tiles(kv[:, s], 2))
    val = np.concatenate([kv[:, 3], kv[:, 5]], 1).reshape(4, 2, P, 512).transpose(0, 2, 1, 3).reshape(4, P, PW)
    w1 = np.asarray(cmp_w1).reshape(2, 2, 8, P, P).transpose(0, 1, 3, 2, 4).reshape(4, P, PW)
    qg = np.asarray(b_w_qg)[0]
    heads = [head_of(e) for e in range(HEADS)]
    q = tiles(qg[:, :hd].reshape(D, HEADS, HD)[:, heads].reshape(D, hd), 8)
    g = np.zeros((P, PW), qg.dtype)
    g[:, :8 * 3 * HEADS] = qg[:, hd:].reshape(KT, P, 3 * HEADS).transpose(1, 0, 2).reshape(P, -1)
    sets = {"cmp": kv_tiles(0) + kv_tiles(1), "key": kv_tiles(2) + kv_tiles(4), "val": list(val), "w1": list(w1),
            "gate": [g], "q": list(q)}
    b_up = np.stack([sets[what][t] for what, t in B_ORDER])
    b_down = np.asarray(b_w_o)[0].reshape(HEADS, HD, D)[heads].reshape(8, P, PW)
    arrays = {
        "xT": np.asarray(x)[0].T.reshape(KT, P, T).transpose(1, 0, 2), "par": par, "hot": one_hot_of_distances(),
        "rel": rel_bias, "a_up": a_up, "a_down": np.asarray(a_w_out)[0].reshape(AU, P, PW), "f_up": f_up,
        "f_down": np.asarray(ffn_down).reshape(2, FU, P, PW), "b_up": b_up, "b_down": b_down,
    }
    arrays = {k: c(v) for k, v in arrays.items()}
    nc = bacc.Bacc("TRN2", target_bir_lowering=False, num_devices=1)
    args = [nc.dram_tensor(f"in_{k}", v.shape, F32, kind="ExternalInput").ap() for k, v in arrays.items()]
    scratch = nc.dram_tensor("bias_rows", [HEADS, 384], F32, kind="Internal").ap()
    out = nc.dram_tensor("out", (P, KT, T), F32, kind="ExternalOutput").ap()
    build(nc, *args, scratch, out)
    r = run(nc, [{f"in_{k}": v for k, v in arrays.items()}], core_ids=[0])
    return c(r.results[0]["out"].transpose(2, 1, 0)).reshape(1, T, D)
```

```python
import math
from contextlib import ExitStack

import numpy as np

import concourse.bass as bass
from concourse import mybir

ALU = mybir.AluOpType
ACT = mybir.ActivationFunctionType
F32 = mybir.dt.float32
F32R = mybir.dt.float32r

P = 128
D = 1024
T = 256
KT = D // P
F = 2816
FU = F // P
AU = D // P
HEADS = 16
GROUPS = 4
HPG = HEADS // GROUPS
HD = 64
CL, CS = 32, 16
NC = (T - CL) // CS + 1
BUCKETS = 32
MAXD = 128
EPS = 1e-6
NEG = -1e30
PW = 1024

PAR = {}
_at = 0
for _name, _n in (("gains", 6 * KT), ("a_taps", 3 * AU), ("f_taps", 2 * 2 * FU * 3), ("pe", 2 * 16),
                  ("b1", 2), ("w2", 2 * HD)):
    PAR[_name] = _at
    _at += _n
NPAR = _at
GAIN = {"mix0": 0, "ffn0": 1, "kv": 2, "mix1": 3, "ffn1": 4, "final": 5}

B_ORDER = ([("cmp", t) for t in range(4)] + [("key", t) for t in range(4)] + [("val", t) for t in range(4)]
           + [("w1", 0), ("gate", 0), ("w1", 1), ("q", 0), ("w1", 2), ("q", 1), ("w1", 3)] + [("q", t) for t in range(2, 8)]
           + [("o", t) for t in range(8)])
NB = len(B_ORDER)
UP_SLOTS, DOWN_SLOTS = 6, 3
AHEAD = 6
O_FIRST = B_ORDER.index(("o", 0))
Q_BEFORE = 5
Q_ROUND = {1: 5, 4: 6, 7: 7}


def q_index(t):
    return B_ORDER.index(("q", t))


NC0 = (P - CL) // CS + 1


def plan_pieces():
    order = [("a", "up", u, c) for u in range(AU) for c in range(3)]
    order += [("f0", "up", u, c) for u in range(FU) for c in range(2)]
    order += [("b", "up", b, 0) for b in range(NB)]
    order += [("f1", "up", u, c) for u in range(FU) for c in range(2)]
    downs = [("a", "down", u, 0) for u in range(AU)] + [("f0", "down", u, 0) for u in range(FU)]
    downs += [("f1", "down", u, 0) for u in range(FU)]
    table = {}
    for keys in (order, downs):
        used, turns = {}, {}
        for n, key in enumerate(keys):
            st, kind, u, c = key
            if kind == "up":
                slot = {"a": 3 * (u % 2) + c, "b": (u + 2) % 6}.get(st, 2 * (u % 3) + c)
            else:
                slot = UP_SLOTS + (u % 2 if st == "a" else u % 3)
            turns[slot] = turns.get(slot, 0) + 1
            table[key] = dict(n=n, slot=slot, turn=turns[slot], prev=used.get(slot))
            used[slot] = n
    return table


def bucket_of(dist):
    half = BUCKETS // 2
    if dist < half:
        return dist
    large = half + int(np.float32(np.log(np.float32(dist) / np.float32(half))) / np.float32(math.log(MAXD / half))
                       * np.float32(BUCKETS - half))
    return min(large, BUCKETS - 1)


def one_hot_of_distances():
    hot = np.zeros((BUCKETS + 1, 512), np.float32)
    for m in range(511):
        hot[bucket_of(255 - m) if m <= 255 else BUCKETS, m] = 1.0
    return hot


def build(nc, xT, par, hot, rel, a_up, a_down, f_up, f_down, b_up, b_down, scratch, out):
    piece = plan_pieces()
    ctx = ExitStack()
    with ctx:
        def sb(name, shape, dt=F32):
            return ctx.enter_context(nc.sbuf_tensor(name, shape, dt))

        def sem(name):
            return ctx.enter_context(nc.semaphore(name))

        x = sb("x", [P, KT, T])
        gx = sb("gx", [P, 2, KT * T], F32R)
        gx_hi, gx_lo = (gx[:, n, :].rearrange("p (k t) -> p k t", k=KT) for n in range(2))
        gq_hi = sb("gq_hi", [P, KT, T], F32R)
        gq_lo = sb("gq_lo", [P, KT, T], F32R)
        w_hi = sb("w_hi", [P, UP_SLOTS + DOWN_SLOTS, PW], F32R)
        w_lo = sb("w_lo", [P, UP_SLOTS + DOWN_SLOTS, PW], F32R)
        staged = sb("staged", [P, UP_SLOTS + 1, PW])
        bias = sb("bias", [P, HEADS, T])
        y = sb("y", [P, 2, 16 * 4 * NC], F32R)
        y_hi, y_lo = y[:, 0, :], y[:, 1, :]
        params = sb("params", [P, NPAR])
        rstd = sb("rstd", [P, T])
        sumsq = sb("sumsq", [P, 2, T])
        ones = sb("ones", [P, P])
        ident = sb("ident", [P, P])
        eps = sb("eps", [P, 1])
        small = sb("small", [P, 320])
        work = sb("work", [P, 8560])

        def part(at, n, rows=P):
            return work[0:rows, at:at + n]

        shifted = part(0, 3 * 2 * 258).rearrange("p (r c t) -> p r c t", r=3, c=2)
        conv = part(1548, 3 * 2 * T).rearrange("p (r c t) -> p r c t", r=3, c=2)
        squares = part(3084, 1024).rearrange("p (b n) -> p b n", b=2)
        deviation = part(4108, T)
        hot_sb = part(4400, 512, BUCKETS + 1)
        table_sb = part(5424, HEADS, BUCKETS + 1)
        rows_sb = part(5440, 384, HEADS)
        rstd2 = part(5840, T)
        tokens = part(0, 2048).rearrange("p (j g t) -> p j g t", j=2, g=GROUPS)
        block_in = part(2048, 16 * 4 * NC)
        gelu = part(3008, 5 * 120).rearrange("p (k n) -> p k n", k=5)
        gateT = part(3616, T, 3 * HEADS)
        NS = 800
        soft = part(0, 3 * NS).rearrange("p (r n) -> p r n", r=3)
        probsT = part(3 * NS, 2 * 1024).rearrange("p (r n) -> p r n", r=2)
        Q0 = 3 * NS + 2048
        qT = part(Q0, 8 * T).rearrange("p (i t) -> p i t", i=8)
        keysT = part(Q0 + 2048, 4 * T).rearrange("p (a b t) -> p a b t", a=2, b=2)
        vals = part(Q0 + 3072, 2 * 512).rearrange("p (k n) -> p k n", k=2)
        assert Q0 + 4096 <= 8560
        kcT = small[:, 0:2 * NC].rearrange("p (a c) -> p a c", a=2)
        vc = small[0:NC, 2 * NC + 2:2 * NC + 2 + GROUPS * HD]
        stats = sb("stats", [P, 3, 24])
        gate = sb("gate", [P, 2, 3 * HEADS])
        rowmask = sb("rowmask", [P, 1])
        rstd_t = sb("rstd_t", [P, 4])
        tiny = sb("tiny", [P, 1])

        bank = [ctx.enter_context(nc.psum_tensor(f"bank{i}", [P, 512], F32)) for i in range(8)]

        landed = [sem(f"landed{s}") for s in range(UP_SLOTS + 1)]
        x_landed = [sem(f"x_landed{b}") for b in range(4)]
        par_landed, hot_landed, bias_landed = sem("par_landed"), sem("hot_landed"), sem("bias_landed")
        hi_up, lo_up, used_up = sem("hi_up"), sem("lo_up"), sem("used_up")
        hi_down, lo_down, used_down = sem("hi_down"), sem("lo_down"), sem("used_down")
        scaled, tapped, convolved, silued, y_done, y_hi_done, y_lo_done = (
            {s: sem(f"{n}_{s}") for s in ("a", "f0", "f1")}
            for n in ("scaled", "tapped", "convolved", "silued", "y_done", "y_hi_done", "y_lo_done"))
        acc_done, x_new = sem("acc_done"), sem("x_new")
        gx_hi_done, gx_lo_done = sem("gx_hi_done"), sem("gx_lo_done")
        gq_hi_done, gq_lo_done = sem("gq_hi_done"), sem("gq_lo_done")
        squared, summed, norm_summed = sem("squared"), sem("summed"), sem("norm_summed")
        deviated, rstd_done, padded = sem("deviated"), sem("rstd_done"), sem("padded")
        consts_done, table_done, rows_done, rows_copied = sem("consts_done"), sem("table_done"), sem("rows_done"), sem("rows_copied")
        rows_stored = sem("rows_stored")
        b_evacuated, tokens_shifted, block_done = sem("b_evacuated"), sem("tokens_shifted"), sem("block_done")
        block_hi_done, block_lo_done = sem("block_hi_done"), sem("block_lo_done")
        vals_done, gate_read, gate_exp, gate_turned, gate_step, gate_done = (
            sem("vals_done"), sem("gate_read"), sem("gate_exp"), sem("gate_turned"), sem("gate_step"), sem("gate_done"))
        pre_gelu, gelu_step, gelu_tanh, hidden_done = sem("pre_gelu"), sem("gelu_step"), sem("gelu_tanh"), sem("hidden_done")
        cmp_mm, cmp_done = sem("cmp_mm"), sem("cmp_done")
        scored, biased, maxed, exped = sem("scored"), sem("biased"), sem("maxed"), sem("exped")
        recipd, weighted, normed, normed_far = sem("recipd"), sem("weighted"), sem("normed"), sem("normed_far")
        turned0, turned1, probs0, probs1 = sem("turned0"), sem("turned1"), sem("probs0"), sem("probs1")
        headed, o_hi_done, o_lo_done = sem("headed"), sem("o_hi_done"), sem("o_lo_done")
        zeroed = sem("zeroed")
        out_done, stored = sem("out_done"), sem("stored")

        NORM = {"a": 0, "f0": 1, "b": 2, "f1": 3, "end": 4}
        GAIN_OF = {"a": "mix0", "f0": "ffn0", "b": "kv", "f1": "ffn1"}
        LAST_PIECE = {"f0": (used_down, piece[("a", "down", AU - 1, 0)]["n"]), "b": (used_down, piece[("f0", "down", FU - 1, 0)]["n"]),
                      "f1": (used_up, piece[("b", "up", NB - 1, 0)]["n"]), "end": (used_down, piece[("f1", "down", FU - 1, 0)]["n"])}
        RSTD_AT = {"a": 2, "f0": 3, "b": 5, "f1": 6, "end": 7}

        def looped(i):
            return not isinstance(i, int)

        ROUNDS = 6

        def gain(name, kt):
            at = PAR["gains"] + GAIN[name] * KT + kt
            return params[:, at:at + 1]

        def tap(st, c, i, k, ring, which):
            if st == "a":
                at = PAR["a_taps"] + 3 * k + which + 3 * ring * i
            else:
                at = PAR["f_taps"] + 3 * ((int(st[1]) * 2 + c) * FU + k) + which + 3 * ring * i
            return params[:, bass.ds(at, 1)]

        def piece_of(st, kind, k, c):
            return piece[(st, kind, k, c)]

        def before(q, st, kind):
            if st[0] == "f" and kind == "down":
                return max(-1 if q["prev"] is None else q["prev"], q["n"] - DOWN_SLOTS)
            return q["prev"]

        def stride(st, kind):
            return {"a": {"up": 6, "down": 2}}.get(st, {"up": 6, "down": 3})[kind]

        blocks = [y[:], gx[:, :, 0:16 * 4 * NC]]
        hidden = [bank[6], bank[3]]

        def pair_bank(b):
            return bank[b // 2 % 3][:, b % 2 * T:(b % 2 + 1) * T]

        def q_bank(t):
            return bank[{0: 1, 1: 0, 2: 2}.get(t, 7)][:, 0:T]

        block = ctx.enter_context(nc.Block())

        @block.sync
        def _(sp):
            def load(st, kind, k, c, i=0):
                q = piece_of(st, kind, k, c)
                move = stride(st, kind) * i
                ring = 2 if st == "a" else 3
                s = min(q["slot"], UP_SLOTS)
                if kind == "up":
                    if q["prev"] is not None:
                        sp.wait_ge(lo_up, q["prev"] + 1 + move)
                elif q["n"] > 0:
                    sp.wait_ge(lo_down, q["n"] + move)
                unit = k + ring * i
                if st == "a":
                    src = a_up[unit, c] if kind == "up" else a_down[unit]
                elif st == "b":
                    src = b_up[k] if k < O_FIRST else b_down[k - O_FIRST]
                else:
                    src = f_up[int(st[1]), unit, c] if kind == "up" else f_down[int(st[1]), unit]
                n = 8 * 3 * HEADS if st == "b" and B_ORDER[k][0] == "gate" else PW
                sp.dma_start(staged[:, s, 0:n], src[:, 0:n]).then_inc(landed[s], 16)

            def ups(st, k, i=0):
                for c in range(3 if st == "a" else 2):
                    load(st, "up", k, c, i)

            ups("a", 0)
            ups("a", 1)
            load("a", "down", 0, 0)
            with sp.Fori(0, AU // 2 - 1) as i:
                for k in (2, 3):
                    ups("a", k, i)
                    load("a", "down", k - 1, 0, i)
            load("a", "down", AU - 1, 0)
            for st in ("f0", "f1"):
                ups(st, 0)
                load(st, "down", 0, 0)
                ups(st, 1)
                ups(st, 2)
                with sp.Fori(0, ROUNDS) as i:
                    for k in (3, 4, 5):
                        ups(st, k, i)
                        load(st, "down", k - 2, 0, i)
                ups(st, FU - 1)
                for k in range(FU - 3, FU):
                    load(st, "down", k, 0)
                if st == "f0":
                    for b in range(NB):
                        load("b", "up", b, 0)
            for b in range(4):
                sp.wait_ge(out_done, 2 * b + 2)
                sp.dma_start(out[:, 2 * b:2 * b + 2, :], x[:, 2 * b:2 * b + 2, :]).then_inc(stored, 16)
            sp.wait_ge(stored, 64)

        @block.gpsimd
        def _(pool):
            nc.gpsimd.memset(ones[:], 1.0).then_inc(consts_done, 1)
            nc.gpsimd.memset(ident[:], 0.0).then_inc(consts_done, 1)
            nc.gpsimd.memset(eps[:], EPS).then_inc(consts_done, 1)
            nc.gpsimd.memset(rowmask[:], 1.0).then_inc(consts_done, 1)
            pool.wait_ge(consts_done, 4)
            nc.gpsimd.affine_select(out=ident[:], in_=ident[:], compare_op=ALU.not_equal, fill=1.0, base=0,
                                    pattern=[[-1, P]], channel_multiplier=1).then_inc(consts_done, 1)
            nc.gpsimd.affine_select(out=rowmask[:], in_=rowmask[:], compare_op=ALU.is_ge, fill=0.0, base=P - CL,
                                    pattern=[[0, 1]], channel_multiplier=-1).then_inc(consts_done, 1)

            def norm(st):
                k = NORM[st]
                for b in range(1, 3):
                    pool.wait_ge(squared, 4 * k + b + 1)
                    if b > 1:
                        pool.wait_ge(summed, 2 * k + 1)
                    total = sumsq[:].rearrange("p h t -> p (h t)")
                    nc.gpsimd.tensor_tensor(total, total, squares[:, b % 2, :], ALU.add).then_inc(summed, 1)

            def pads(n):
                nc.gpsimd.memset(shifted[:, :, :, 0:2], 0.0).then_inc(padded, 1)

            pads(0)
            norm("a")
            pool.wait_ge(rows_copied, 1)
            pool.dma_start(scratch, rows_sb).then_inc(rows_stored, 16)
            pool.wait_ge(rows_stored, 16)
            diagonals = bass.AP(tensor=scratch.tensor, offset=0, ap=[[1, P], [384, HEADS], [1, T]])
            pool.dma_start(bias[:], diagonals).then_inc(bias_landed, 16)
            norm("f0")
            norm("b")
            for j in range(2):
                pool.wait_ge(tokens_shifted, j + 1)
                if j:
                    pool.wait_ge(block_lo_done, 1)
                tok, pe_j = tokens[:, j, 0, 0:1], params[:, PAR["pe"] + 16 * j:PAR["pe"] + 16 * j + 16]
                tok = bass.AP(tensor=tok.tensor, offset=tok.offset, ap=[tok.ap[0], [2, 16], [T, GROUPS], [CS, NC]])
                pe_j = pe_j.unsqueeze(2).unsqueeze(3).to_broadcast([P, 16, GROUPS, NC])
                nc.gpsimd.tensor_tensor(block_in.rearrange("p (i g c) -> p i g c", i=16, g=GROUPS), tok, pe_j,
                                        ALU.add).then_inc(block_done, 1)
                pool.wait_ge(block_hi_done, j + 1)
                nc.gpsimd.tensor_tensor(blocks[j][:, 1, :], block_in, blocks[j][:, 0, :].bitcast(F32),
                                        ALU.subtract).then_inc(block_lo_done, 1)
            pool.wait_ge(block_lo_done, 2)
            nc.gpsimd.memset(soft[:, :, NC0:NC], 0.0).then_inc(zeroed, 1)
            for e in range(HEADS):
                pool.wait_ge(weighted, e + 1)
                for n in NARROW:
                    at, w = SPANS[n]
                    q = nc.gpsimd.tensor_scalar(soft[:, e % 3, at:at + w], soft[:, e % 3, at:at + w],
                                                stats[:, e % 3, 18 + n:19 + n], None, ALU.mult)
                q.then_inc(normed, 1)
            pool.wait_ge(headed, HEADS)
            pads(1)
            norm("f1")
            norm("end")

        @block.scalar
        def _(act):
            act.dma_start(hot_sb, hot).then_inc(hot_landed, 16)
            act.dma_start(table_sb[0:BUCKETS, :], rel).then_inc(hot_landed, 16)
            act.dma_start(params[:], par).then_inc(par_landed, 16)
            for b in range(4):
                act.dma_start(x[:, 2 * b:2 * b + 2, :], xT[:, 2 * b:2 * b + 2, :]).then_inc(x_landed[b], 16)

            def lead(st, kind, k, c, i=0):
                q = piece_of(st, kind, k, c)
                move = stride(st, kind) * i
                s = min(q["slot"], UP_SLOTS)
                hi, used = (hi_up, used_up) if kind == "up" else (hi_down, used_down)
                if kind == "up":
                    act.wait_ge(landed[s], 16 * q["turn"] + 16 * i)
                else:
                    act.wait_ge(landed[s], 16 * (q["n"] + 1) + 16 * move)
                last = before(q, st, kind)
                if last is not None and last >= 0:
                    act.wait_ge(used, last + 1 + move)
                n = 8 * 3 * HEADS if st == "b" and B_ORDER[k][0] == "gate" else PW
                nc.scalar.activation(w_hi[:, q["slot"], 0:n], staged[:, s, 0:n], ACT.Copy).then_inc(hi, 1)

            def norm(st, first=False, meanwhile=()):
                k = NORM[st]
                for b in range(4):
                    if first:
                        act.wait_ge(x_landed[b], 16)
                    else:
                        act.wait_ge(x_new, 4 * (k - 1) + b + 1)
                    if first and b == 0:
                        act.wait_ge(par_landed, 16)
                    if st != "end":
                        for kt in (2 * b, 2 * b + 1):
                            nc.scalar.activation(gx_hi[:, kt, :], x[:, kt, :], ACT.Copy,
                                                 scale=gain(GAIN_OF[st], kt)).then_inc(gx_hi_done, 1)
                    if b == 3:
                        act.wait_ge(summed, 2 * k + 1)
                    dst = sumsq[:].rearrange("p h t -> p (h t)") if b == 0 else squares[:, b % 2, :]
                    nc.scalar.activation(dst, x[:, 2 * b:2 * b + 2, :].rearrange("p k t -> p (k t)"),
                                         ACT.Square).then_inc(squared, 1)
                nc.scalar.activation(tiny[:, 0:1], eps[:], ACT.Sqrt)
                for q in meanwhile:
                    lead(*q)
                act.wait_ge(norm_summed, k + 1)
                q = nc.scalar.activation(deviation, bank[3][:, 0:T], ACT.Sqrt, bias=eps[:], scale=1.0 / D)
                if st == "b":
                    q = nc.scalar.activation(rstd_t[:, 2:4], bank[3][:, T:T + 2], ACT.Sqrt, bias=eps[:], scale=1.0 / D)
                q.then_inc(deviated, 1)

            def step(st, k, ahead, i=0):
                ring = 2 if st == "a" else 3
                r = k % ring
                u = k + ring * i
                early, middle, late = ahead
                for q in early:
                    lead(*q)
                for c in range(1 if st == "a" else 2):
                    if c == 0:
                        act.wait_ge(scaled[st], u + 1)
                    nc.scalar.activation(conv[:, r, c, :], shifted[:, r, c, 2:2 + T], ACT.Copy,
                                         scale=tap(st, c, i, k, ring, 2)).then_inc(tapped[st], 1)
                for q in middle:
                    lead(*q)
                if st != "a":
                    act.wait_ge(convolved[st], 4 * u + 3)
                    nc.scalar.activation(conv[:, r, 0, :], conv[:, r, 0, :], ACT.Silu).then_inc(silued[st], 1)
                act.wait_ge(y_done[st], u + 1)
                q = piece_of(st, "down", k, 0)
                back = {"a": 2, "f0": 3, "f1": 3}[st]
                if k >= back or looped(i):
                    act.wait_ge(used_down, q["n"] - back + 1 + stride(st, "down") * i)
                nc.scalar.activation(y_hi[:, r * T:(r + 1) * T], conv[:, r, 1, :], ACT.Copy).then_inc(y_hi_done[st], 1)
                for q in late:
                    lead(*q)

            def stage(st, nxt):
                if st == "a":
                    step(st, 0, AHEAD_A(0))
                    step(st, 1, AHEAD_A(1))
                    with act.Fori(0, 2) as i:
                        for k in (2, 3):
                            step(st, k, AHEAD_A(k, i), i)
                else:
                    step(st, 0, ([(st, "down", 1, 0)], [], []))
                    with act.Fori(0, ROUNDS) as i:
                        for k in (1, 2, 3):
                            step(st, k, AHEAD_F(st, k, i), i)
                    step(st, 19, AHEAD_F(st, 19))
                units = AU if st == "a" else FU
                step(st, units - 2, (nxt[0][0:1], nxt[0][1:2], [(st, "down", units - 1, 0)]))
                step(st, units - 1, ([], [], nxt[1]))

            lead("a", "up", 0, 0)
            norm("a", first=True, meanwhile=START_A)
            stage("a", [UPS("f0", 0), UPS("f0", 1)])
            norm("f0", meanwhile=UPS("f0", 2))
            lead("f0", "down", 0, 0)
            stage("f0", [B_PIECES(0, 2), B_PIECES(2, 4)])
            norm("b", meanwhile=B_PIECES(4, 6))
            for kt in range(KT):
                nc.scalar.activation(gq_hi[:, kt, :], x[:, kt, :], ACT.Copy, scale=gain("mix1", kt)).then_inc(gq_hi_done, 1)

            UB = piece[("b", "up", 0, 0)]["n"]
            for b, (what, t) in enumerate(B_ORDER):
                if b in (2, 4):
                    j = b // 2 - 1
                    act.wait_ge(b_evacuated, 2 * j + 2)
                    nc.scalar.activation(tokens[HD:P, j, :, 0:T - 1], tokens[0:HD, j, :, 1:T], ACT.Copy).then_inc(tokens_shifted, 1)
                if b in (6, 12):
                    j = 0 if b == 6 else 1
                    act.wait_ge(block_done, j + 1)
                    if j:
                        act.wait_ge(used_up, UB + B_ORDER.index(("val", 3)) + 1)
                    nc.scalar.activation(blocks[j][:, 0, :], block_in, ACT.Copy).then_inc(block_hi_done, 1)
                if what == "val" and t == 3:
                    act.wait_ge(used_up, UB + b + 1)
                    act.wait_ge(rstd_done, RSTD_AT["b"])
                    for k in range(2):
                        nc.scalar.activation(vals[:, k, :], bank[4 + k][:], ACT.Copy, scale=rstd_t[:, k:k + 1]).then_inc(vals_done, 1)
                if what == "gate":
                    act.wait_ge(gate_read, 1)
                    nc.scalar.activation(gateT, gateT, ACT.Exp).then_inc(gate_exp, 1)
                if (what, t) == ("q", 2):
                    act.wait_ge(gelu_step, 3)
                    nc.scalar.activation(gelu[:, 3, :], gelu[:, 2, :], ACT.Tanh, scale=math.sqrt(2 / math.pi)).then_inc(gelu_tanh, 1)
                lead("b", "up", b + AHEAD, 0)
                if (what, t) == ("q", Q_BEFORE - 1):
                    break

            for e in range(HEADS + 4):
                if e >= 5 and e % 2 == 1:
                    i = (e - 5) // 2
                    act.wait_ge(headed, 2 * i + 2)
                    nc.scalar.activation(gx_hi[:, i, :].rearrange("p (k t) -> p k t", k=2), backwards(bank[6][:, 0:T]),
                                         ACT.Copy).then_inc(o_hi_done, 1)
                if e < HEADS:
                    act.wait_ge(maxed, e + 1)
                    if e >= 3:
                        act.wait_ge(recipd, e - 2)
                    for n, (at, w) in enumerate(SPANS):
                        q = nc.scalar.activation(soft[:, e % 3, at:at + w], soft[:, e % 3, at:at + w], ACT.Exp,
                                                 bias=stats[:, e % 3, 6 + n:7 + n], accum_out=stats[:, e % 3, 12 + n:13 + n])
                    q.then_inc(exped, 1)
                if 2 <= e < HEADS + 2:
                    h = e - 2
                    act.wait_ge(turned0, h + 1)
                    if h >= 2:
                        act.wait_ge(headed, h - 1)
                    nc.scalar.activation(probsT[:, h % 2, 0:512], bank[4][:], ACT.Copy).then_inc(probs0, 1)
                if e in Q_ROUND:
                    lead("b", "up", q_index(Q_ROUND[e]) + AHEAD, 0)
            for q in WHILE_O:
                lead(*q)
            norm("f1", meanwhile=UPS("f1", 2))
            lead("f1", "down", 0, 0)
            stage("f1", [[], []])
            norm("end")

        @block.vector
        def _(dve):
            def rest(st, kind, k, c, i=0):
                q = piece_of(st, kind, k, c)
                move = stride(st, kind) * i
                s = min(q["slot"], UP_SLOTS)
                hi, lo = (hi_up, lo_up) if kind == "up" else (hi_down, lo_down)
                dve.wait_ge(hi, q["n"] + 1 + move)
                n = 8 * 3 * HEADS if st == "b" and B_ORDER[k][0] == "gate" else PW
                nc.vector.tensor_tensor(w_lo[:, q["slot"], 0:n], staged[:, s, 0:n], w_hi[:, q["slot"], 0:n].bitcast(F32),
                                        ALU.subtract).then_inc(lo, 1)

            def norm(st, first=False, meanwhile=()):
                k = NORM[st]

                def residual(b):
                    if b < 3:
                        dve.wait_ge(acc_done, 3 * (k - 1) + b + 1)
                    else:
                        done, n = LAST_PIECE[st]
                        dve.wait_ge(done, n + 1)
                    xb = x[:, 2 * b:2 * b + 2, :].rearrange("p k t -> p (k t)")
                    nc.vector.tensor_tensor(xb, xb, bank[4 + b][:], ALU.add).then_inc(x_new, 1)

                if not first:
                    residual(0)
                    residual(1)
                for b in range(4):
                    if st != "end":
                        for kt in (2 * b, 2 * b + 1):
                            dve.wait_ge(gx_hi_done, 8 * k + kt + 1)
                            if first:
                                dve.wait_ge(par_landed, 16)
                                dve.wait_ge(x_landed[b], 16)
                            nc.vector.scalar_tensor_tensor(gx_lo[:, kt, :], x[:, kt, :], gain(GAIN_OF[st], kt),
                                                           gx_hi[:, kt, :].bitcast(F32), ALU.mult, ALU.subtract).then_inc(gx_lo_done, 1)
                    if not first and b < 2:
                        residual(b + 2)
                for q in meanwhile:
                    rest(*q)
                dve.wait_ge(deviated, k + 1)
                nc.vector.reciprocal(rstd[:], deviation).then_inc(rstd_done, 1)
                if st == "a":
                    dve.wait_ge(rstd_done, 1)
                    nc.vector.tensor_tensor(rstd2, rstd[:], rstd[:], ALU.mult).then_inc(rstd_done, 1)
                elif st == "b":
                    nc.vector.reciprocal(rstd_t[:, 0:2], rstd_t[:, 2:4]).then_inc(rstd_done, 1)
                dve.wait_ge(rstd_done, RSTD_AT[st])

            def step(st, k, ahead, i=0):
                ring = 2 if st == "a" else 3
                r = k % ring
                u = k + ring * i
                early, middle, late = ahead
                last = piece_of(st, "up", k, 2 if st == "a" else 1)
                dve.wait_ge(used_up, last["n"] + 1 + stride(st, "up") * i)
                if st == "a":
                    nc.vector.tensor_tensor(shifted[:, r, 1, 2:2 + T], bank[2 * r][:, 0:T], rstd[:], ALU.mult)
                    nc.vector.tensor_tensor(conv[:, r, 1, :], bank[2 * r][:, T:2 * T], rstd2, ALU.mult).then_inc(convolved[st], 1)
                    dve.wait_ge(convolved[st], 3 * u + 1)
                    nc.vector.tensor_tensor(shifted[:, r, 0, 2:2 + T], bank[2 * r + 1][:, 0:T], conv[:, r, 1, :],
                                            ALU.mult).then_inc(scaled[st], 1)
                    halves, per, off = 1, 3, 1
                else:
                    nc.vector.tensor_tensor(shifted[:, r, :, 2:2 + T], bank[r][:].rearrange("p (c t) -> p c t", c=2),
                                            rstd[:].unsqueeze(1).to_broadcast([P, 2, T]), ALU.mult).then_inc(scaled[st], 1)
                    halves, per, off = 2, 4, 0
                for q in early:
                    rest(*q)
                for c in range(halves):
                    dve.wait_ge(tapped[st], halves * u + c + 1)
                    nc.vector.scalar_tensor_tensor(conv[:, r, c, :], shifted[:, r, c, 1:1 + T], tap(st, c, i, k, ring, 1),
                                                   conv[:, r, c, :], ALU.mult, ALU.add).then_inc(convolved[st], 1)
                for c in range(halves):
                    dve.wait_ge(convolved[st], per * u + off + c + 1)
                    nc.vector.scalar_tensor_tensor(conv[:, r, c, :], shifted[:, r, c, 0:T], tap(st, c, i, k, ring, 0),
                                                   conv[:, r, c, :], ALU.mult, ALU.add).then_inc(convolved[st], 1)
                for q in middle:
                    rest(*q)
                dve.wait_ge(convolved[st], per * u + per)
                if st == "a":
                    nc.vector.tensor_tensor(conv[:, r, 1, :], conv[:, r, 0, :], shifted[:, r, 1, 2:2 + T],
                                            ALU.mult).then_inc(y_done[st], 1)
                else:
                    dve.wait_ge(silued[st], u + 1)
                    nc.vector.tensor_tensor(conv[:, r, 1, :], conv[:, r, 0, :], conv[:, r, 1, :],
                                            ALU.mult).then_inc(y_done[st], 1)
                dve.wait_ge(y_hi_done[st], u + 1)
                nc.vector.tensor_tensor(y_lo[:, r * T:(r + 1) * T], conv[:, r, 1, :], y_hi[:, r * T:(r + 1) * T].bitcast(F32),
                                        ALU.subtract).then_inc(y_lo_done[st], 1)
                for q in late:
                    rest(*q)

            def stage(st, nxt):
                if st == "a":
                    step(st, 0, AHEAD_A(0))
                    step(st, 1, AHEAD_A(1))
                    with dve.Fori(0, 2) as i:
                        for k in (2, 3):
                            step(st, k, AHEAD_A(k, i), i)
                else:
                    step(st, 0, ([(st, "down", 1, 0)], [], []))
                    with dve.Fori(0, ROUNDS) as i:
                        for k in (1, 2, 3):
                            step(st, k, AHEAD_F(st, k, i), i)
                    step(st, 19, AHEAD_F(st, 19))
                units = AU if st == "a" else FU
                step(st, units - 2, (nxt[0][0:1], nxt[0][1:2], [(st, "down", units - 1, 0)]))
                step(st, units - 1, ([], [], nxt[1]))

            nc.vector.memset(table_sb[BUCKETS:BUCKETS + 1, :], NEG).then_inc(table_done, 1)
            dve.wait_ge(rows_done, 1)
            nc.vector.tensor_copy(rows_sb, bank[4][0:HEADS, 0:384]).then_inc(rows_copied, 1)

            rest("a", "up", 0, 0)
            norm("a", first=True, meanwhile=START_A)
            dve.wait_ge(padded, 1)
            stage("a", [UPS("f0", 0), UPS("f0", 1)])
            norm("f0", meanwhile=UPS("f0", 2))
            rest("f0", "down", 0, 0)
            stage("f0", [B_PIECES(0, 2), B_PIECES(2, 4)])
            norm("b", meanwhile=B_PIECES(4, 6))

            UB = piece[("b", "up", 0, 0)]["n"]

            def query(t):
                dve.wait_ge(used_up, UB + q_index(t) + 1)
                nc.vector.scalar_tensor_tensor(backwards(qT[:, t, :]), q_bank(t).rearrange("p (k t) -> p k t", k=2), HD ** -0.5,
                                               rstd[:].rearrange("p (k t) -> p k t", k=2), ALU.mult, ALU.mult).then_inc(b_evacuated, 1)

            for b, (what, t) in enumerate(B_ORDER):
                if what in ("cmp", "key"):
                    dve.wait_ge(used_up, UB + b // 2 * 2 + 2)
                    src = pair_bank(b)
                if what == "cmp":
                    j, a = t // 2, t % 2
                    for p in range(2):
                        q = nc.vector.tensor_tensor(tokens[0:HD, j, 2 * a + p, :], src[HD * p:HD * p + HD, :],
                                                    rstd[0:HD, :], ALU.mult)
                    q.then_inc(b_evacuated, 1)
                elif what == "key":
                    nc.vector.tensor_tensor(keysT[:, t % 2, t // 2, :], src, rstd[:], ALU.mult).then_inc(b_evacuated, 1)
                if what == "key":
                    for kt in (2 * t, 2 * t + 1):
                        dve.wait_ge(gq_hi_done, kt + 1)
                        nc.vector.scalar_tensor_tensor(gq_lo[:, kt, :], x[:, kt, :], gain("mix1", kt), gq_hi[:, kt, :].bitcast(F32),
                                                       ALU.mult, ALU.subtract).then_inc(gq_lo_done, 1)
                if what == "gate":
                    dve.wait_ge(used_up, UB + b + 1)
                    nc.vector.scalar_tensor_tensor(backwards(gateT), bank[7][0:3 * HEADS, 0:T].rearrange("p (k t) -> p k t", k=2),
                                                   -1.0, rstd[0:3 * HEADS, :].rearrange("p (k t) -> p k t", k=2),
                                                   ALU.mult, ALU.mult).then_inc(gate_read, 1)
                if what == "w1" and t in (1, 3):
                    j = t // 2
                    dve.wait_ge(used_up, UB + b + 1)
                    z_j = gelu[:, 0, 60 * j:60 * j + 60]
                    nc.vector.tensor_scalar(z_j, hidden[j][:, 0:60], params[:, PAR["b1"] + j:PAR["b1"] + j + 1], None,
                                            ALU.add).then_inc(pre_gelu, 1)
                    dve.wait_ge(pre_gelu, 2 * j + 1)
                    nc.vector.tensor_tensor(z_j, z_j, hidden[j][:, 60:120], ALU.add).then_inc(pre_gelu, 1)
                if (what, t) == ("w1", 2):
                    dve.wait_ge(gate_turned, 1)
                    dve.wait_ge(consts_done, 6)
                    nc.vector.tensor_scalar(gate[:].rearrange("p k n -> p (k n)"), bank[7][:, T:T + 6 * HEADS], 1.0, None,
                                            ALU.add).then_inc(gate_step, 1)
                    dve.wait_ge(gate_step, 1)
                    nc.vector.reciprocal(gate[:], gate[:]).then_inc(gate_step, 1)
                    dve.wait_ge(gate_step, 2)
                    first = gate[:, 0, 0:3 * HEADS:3]
                    nc.vector.tensor_scalar(first, first, rowmask[:], None, ALU.mult).then_inc(gate_done, 1)
                z, a1, a2, th, hid = (gelu[:, n, :] for n in range(5))
                if (what, t) == ("w1", 3):
                    dve.wait_ge(pre_gelu, 4)
                    nc.vector.tensor_tensor(a1, z, z, ALU.mult).then_inc(gelu_step, 1)
                    dve.wait_ge(gelu_step, 1)
                    nc.vector.tensor_scalar(a1, a1, 0.044715, 1.0, ALU.mult, ALU.add).then_inc(gelu_step, 1)
                    dve.wait_ge(gelu_step, 2)
                    nc.vector.tensor_tensor(a2, a1, z, ALU.mult).then_inc(gelu_step, 1)
                if (what, t) == ("q", 2):
                    dve.wait_ge(gelu_tanh, 1)
                    nc.vector.tensor_scalar(th, th, 1.0, 0.5, ALU.add, ALU.mult).then_inc(gelu_step, 1)
                    dve.wait_ge(gelu_step, 4)
                    nc.vector.tensor_tensor(hid, th, z, ALU.mult).then_inc(hidden_done, 1)
                if what == "q":
                    query(t)
                if (what, t) == ("q", 3):
                    dve.wait_ge(cmp_mm, 1)
                    for p in range(2):
                        nc.vector.tensor_copy(kcT[HD * p:HD * p + HD, :, :],
                                              bank[6][0:HD, 128:128 + 60].rearrange("p (a q c) -> p a q c", a=2, q=2)[:, :, p, :])
                    nc.vector.tensor_copy(vc, bank[6][0:NC, 256:512]).then_inc(cmp_done, 1)
                rest("b", "up", b + AHEAD, 0)
                if (what, t) == ("q", Q_BEFORE - 1):
                    break
            dve.wait_ge(bias_landed, 16)
            dve.wait_ge(gate_done, 1)

            for e in range(HEADS + 4):
                if e < HEADS:
                    h = head_of(e)
                    r = e % 3
                    dve.wait_ge(scored, e + 1)
                    if e >= 3:
                        dve.wait_ge(turned1, e - 2)
                    s0, s1 = bank[2 * (e % 2)], bank[2 * (e % 2) + 1]
                    ends = bias[:, h, CL - 1::CS]
                    near, near_ends = bias[:, h, P:T], bias[:, h, P + CL - 1::CS]
                    srcs = [(s0[:, T:T + NC0], near_ends), (s0[:, T + 16:T + 16 + NC], ends), (s0[:, 0:P], near),
                            (s1[:, 0:T], bias[:, h, :]), (s0[:, P:2 * P], near), (s1[:, T:2 * T], bias[:, h, :])]
                    for n, ((at, w), (sc, bi)) in enumerate(zip(SPANS, srcs)):
                        q = nc.vector.tensor_tensor_reduce(soft[:, r, at:at + w], sc, bi, 1.0, -3.0e38, ALU.add, ALU.max,
                                                           stats[:, r, n:n + 1])
                    q.then_inc(biased, 1)
                    dve.wait_ge(biased, e + 1)
                    nc.vector.tensor_scalar(stats[:, r, 6:12], stats[:, r, 0:6], -1.0, None, ALU.mult).then_inc(maxed, 1)
                if e - 1 in Q_ROUND:
                    query(Q_ROUND[e - 1])
                    rest("b", "up", q_index(Q_ROUND[e - 1]) + AHEAD, 0)
                if e >= 5 and e % 2 == 1:
                    i = (e - 5) // 2
                    dve.wait_ge(o_hi_done, i + 1)
                    nc.vector.tensor_tensor(gx_lo[:, i, :].rearrange("p (k t) -> p k t", k=2), backwards(bank[6][:, 0:T]),
                                            gx_hi[:, i, :].bitcast(F32).rearrange("p (k t) -> p k t", k=2),
                                            ALU.subtract).then_inc(o_lo_done, 1)
                if 1 <= e < HEADS + 1:
                    g, r = e - 1, (e - 1) % 3
                    h = head_of(g)
                    dve.wait_ge(exped, g + 1)
                    nc.vector.reciprocal(stats[:, r, 18:24], stats[:, r, 12:18]).then_inc(recipd, 1)
                    dve.wait_ge(recipd, g + 1)
                    w = stats[:, r, 18:24].rearrange("p (b k) -> p b k", b=3)
                    nc.vector.tensor_tensor(w, w, gate[:, :, 3 * h:3 * h + 3].rearrange("p k b -> p b k"),
                                            ALU.mult).then_inc(weighted, 1)
                    dve.wait_ge(weighted, g + 1)
                    for n in WIDE:
                        at, w = SPANS[n]
                        q = nc.vector.tensor_scalar(soft[:, r, at:at + w], soft[:, r, at:at + w], stats[:, r, 18 + n:19 + n],
                                                    None, ALU.mult)
                    q.then_inc(normed_far, 1)
                if 2 <= e < HEADS + 2:
                    g = e - 2
                    dve.wait_ge(turned1, g + 1)
                    if g >= 2:
                        dve.wait_ge(headed, g - 1)
                    nc.vector.tensor_copy(probsT[:, g % 2, 512:768], bank[5][:, 0:T])
                    nc.vector.tensor_copy(probsT[0:NC, g % 2, 768:1024], bank[5][0:NC, T:2 * T]).then_inc(probs1, 1)
            for q in WHILE_O:
                rest(*q)
            norm("f1", meanwhile=UPS("f1", 2))
            rest("f1", "down", 0, 0)
            dve.wait_ge(padded, 2)
            stage("f1", [[], []])
            norm("end")
            for kt in range(KT):
                nc.vector.scalar_tensor_tensor(x[:, kt, :], x[:, kt, :], gain("final", kt), rstd[:], ALU.mult,
                                               ALU.mult).then_inc(out_done, 1)

        @block.tensor
        def _(pe):
            def three(out_ap, whi, wlo, xhi, xlo, start, stop):
                nc.tensor.matmul(out_ap, whi, xhi, start=start, stop=False, skip_group_check=True)
                nc.tensor.matmul(out_ap, whi, xlo, start=False, stop=False, skip_group_check=True)
                return nc.tensor.matmul(out_ap, wlo, xhi, start=False, stop=stop, skip_group_check=True)

            def product(q, dst, xh, xl, first, move=0, fresh=None, hi_sem=None):
                s = q["slot"]
                pe.wait_ge(lo_up, q["n"] + 1 + move)
                for kt in range(KT):
                    if fresh is not None:
                        pe.wait_ge(fresh, hi_sem + kt + 1)
                    mm = three(dst, w_hi[:, s, kt * P:kt * P + P], w_lo[:, s, kt * P:kt * P + P],
                               xh[:, kt, :], xl[:, kt, :], first and kt == 0, kt == KT - 1)
                mm.then_inc(used_up, 1)

            def up_place(st, k, c):
                if st == "a":
                    b, half = 2 * (k % 2) + c // 2, c % 2
                else:
                    b, half = k % 3, c
                return bank[b][:, half * T:(half + 1) * T], half == 0

            def up(st, k, i=0):
                fresh = (gx_lo_done, 8 * NORM[st]) if k == 0 else (None, None)
                ring = 2 if st == "a" else 3
                if k >= ring:
                    pe.wait_ge(scaled[st], k - ring + 1 + ring * i)
                move = stride(st, "up") * i
                for c in range(3 if st == "a" else 2):
                    dst, first = up_place(st, k, c)
                    product(piece_of(st, "up", k, c), dst, gx_hi, gx_lo, first, move, *fresh)

            def together(st, todo):
                for q, dst, first in todo:
                    pe.wait_ge(lo_up, q["n"] + 1)
                for kt in range(KT):
                    pe.wait_ge(gx_lo_done, 8 * NORM[st] + kt + 1)
                    if kt == KT - 1:
                        norm(st)
                    for q, dst, first in todo:
                        s = q["slot"]
                        mm = three(dst, w_hi[:, s, kt * P:kt * P + P], w_lo[:, s, kt * P:kt * P + P], gx_hi[:, kt, :],
                                   gx_lo[:, kt, :], first and kt == 0, kt == KT - 1)
                        if kt == KT - 1:
                            mm.then_inc(used_up, 1)

            def share(first, last, s, yh, yl):
                for m in range(KT):
                    mm = three(bank[4 + m // 2][:, (m % 2) * T:(m % 2 + 1) * T], w_hi[:, s, m * P:m * P + P],
                               w_lo[:, s, m * P:m * P + P], yh, yl, first and m % 2 == 0, last)
                    if last and m in (1, 3, 5):
                        mm.then_inc(acc_done, 1)
                return mm

            def down(st, k, i=0):
                ring = 2 if st == "a" else 3
                r = k % ring
                q = piece_of(st, "down", k, 0)
                pe.wait_ge(y_lo_done[st], k + 1 + ring * i)
                pe.wait_ge(lo_down, q["n"] + 1 + stride(st, "down") * i)
                first = not looped(i) and k == 0
                last = not looped(i) and k == (AU if st == "a" else FU) - 1
                share(first, last, q["slot"], y_hi[:, r * T:(r + 1) * T], y_lo[:, r * T:(r + 1) * T]).then_inc(used_down, 1)

            def norm(st):
                k = NORM[st]
                pe.wait_ge(summed, 2 * k + 2)
                pe.wait_ge(squared, 4 * k + 4)
                if k == 0:
                    pe.wait_ge(consts_done, 6)
                parts = [sumsq[:, 0, :], sumsq[:, 1, :], squares[:, 1, 0:T], squares[:, 1, T:2 * T]]
                for h, sq in enumerate(parts):
                    mm = nc.tensor.matmul(bank[3][:, 0:T], ones[:], sq, start=h == 0, stop=h == 3, skip_group_check=True)
                if st == "b":
                    for t in range(2):
                        for h, sq in enumerate(parts):
                            mm = nc.tensor.matmul(bank[3][:, T + t:T + t + 1], sq[:, t * P:t * P + P], ones[:, 0:1],
                                                  start=False, stop=h == 3, skip_group_check=True)
                mm.then_inc(norm_summed, 1)

            def stage(st):
                if st == "a":
                    up(st, 0)
                    norm(st)
                    pe.wait_ge(deviated, 1)
                    up(st, 1)
                    down(st, 0)
                    with pe.Fori(0, AU // 2 - 1) as i:
                        for k in (2, 3):
                            up(st, k, i)
                            down(st, k - 1, i)
                    down(st, AU - 1)
                else:
                    together(st, [(piece_of(st, "up", k, c), *up_place(st, k, c)) for k in range(2) for c in range(2)])
                    up(st, 2)
                    down(st, 0)
                    with pe.Fori(0, ROUNDS) as i:
                        for k in (3, 4, 5):
                            up(st, k, i)
                            down(st, k - 2, i)
                    up(st, FU - 1)
                    for k in range(FU - 3, FU):
                        down(st, k)

            pe.wait_ge(hot_landed, 32)
            pe.wait_ge(table_done, 1)
            nc.tensor.matmul(bank[4][0:HEADS, 0:384], table_sb, hot_sb[:, 0:384], start=True, stop=True).then_inc(rows_done, 1)

            stage("a")
            stage("f0")

            UB = piece[("b", "up", 0, 0)]["n"]

            def queries(t):
                if t == 3:
                    pe.wait_ge(gate_done, 1)
                elif t > 3:
                    pe.wait_ge(b_evacuated, 8 + t)
                product(piece_of("b", "up", q_index(t), 0), q_bank(t), gq_hi, gq_lo, True)

            def compressed():
                pe.wait_ge(hidden_done, 1)
                hid = gelu[:, 4, :]
                w2 = params[:, PAR["w2"]:PAR["w2"] + 2 * HD]
                nc.tensor.matmul(bank[6][0:HD, 128:188], w2[:, 0:HD], hid[:, 0:60], start=True, stop=True)
                for g in range(GROUPS):
                    mm = nc.tensor.matmul(bank[6][0:NC, 256 + HD * g:256 + HD * g + HD], hid[:, 60 + NC * g:60 + NC * g + NC],
                                          w2[:, HD:2 * HD], start=True, stop=True)
                mm.then_inc(cmp_mm, 1)

            together("b", [(piece_of("b", "up", b, 0), pair_bank(b), b % 2 == 0) for b in range(4)])
            for b in range(4, q_index(Q_BEFORE - 1) + 1):
                what, t = B_ORDER[b]
                q = piece_of("b", "up", b, 0)
                s = q["slot"]
                if what == "key":
                    if b == 6:
                        pe.wait_ge(b_evacuated, 2)
                    product(q, pair_bank(b), gx_hi, gx_lo, b % 2 == 0)
                    continue
                if what == "q":
                    if t == 0:
                        pe.wait_ge(gq_lo_done, 8)
                        pe.wait_ge(b_evacuated, 8)
                    queries(t)
                    if t == 0:
                        pe.wait_ge(gate_exp, 1)
                        for k in range(2):
                            mm = nc.tensor.transpose(bank[7][:, T + 3 * HEADS * k:T + 3 * HEADS * (k + 1)],
                                                     gateT[:, k * P:k * P + P], ident[0:3 * HEADS, 0:3 * HEADS])
                        mm.then_inc(gate_turned, 1)
                    if t == Q_BEFORE - 2:
                        compressed()
                    continue
                pe.wait_ge(lo_up, q["n"] + 1)
                if what == "val":
                    if t == 0:
                        pe.wait_ge(x_new, 8)
                    for tt in range(2):
                        for kk in range(2):
                            kt = 2 * t + kk
                            mm = three(bank[4 + tt][:], gx_hi[:, kt, tt * P:tt * P + P], gx_lo[:, kt, tt * P:tt * P + P],
                                       w_hi[:, s, kk * 512:kk * 512 + 512], w_lo[:, s, kk * 512:kk * 512 + 512],
                                       kt == 0, kt == KT - 1)
                elif what == "w1":
                    j = t // 2
                    if t % 2 == 0:
                        pe.wait_ge(block_lo_done, j + 1)
                    for i8 in range(8):
                        i = 8 * (t % 2) + i8
                        nc.tensor.matmul(hidden[j][:, 0:120].rearrange("p (a n) -> p a n", a=2), w_hi[:, s, i8 * P:i8 * P + P],
                                         blocks[j][:, :, 60 * i:60 * i + 60], start=i == 0, stop=i == 15, skip_group_check=True)
                        mm = nc.tensor.matmul(hidden[j][:, 0:60], w_lo[:, s, i8 * P:i8 * P + P],
                                              blocks[j][:, 0, 60 * i:60 * i + 60], start=False, stop=i == 15, skip_group_check=True)
                elif what == "gate":
                    pe.wait_ge(gq_lo_done, 8)
                    for kt in range(KT):
                        mm = three(bank[7][0:3 * HEADS, 0:T], w_hi[:, s, 48 * kt:48 * kt + 48], w_lo[:, s, 48 * kt:48 * kt + 48],
                                   gq_hi[:, kt, :], gq_lo[:, kt, :], kt == 0, kt == KT - 1)
                mm.then_inc(used_up, 1)

            def scores(e):
                i, p = e // 2, e % 2
                a = i // HPG
                rows = slice(HD * p, HD * p + HD)
                s0, s1 = bank[2 * p], bank[2 * p + 1]
                pe.wait_ge(b_evacuated, 8 + max(i + 1, 2 + p))
                if e >= 2:
                    pe.wait_ge(biased, e - 1)
                near, far = (qT[rows, i, t * P:t * P + P] for t in range(2))
                nc.tensor.matmul(s0[:, 0:T].rearrange("p (b k) -> p b k", b=2), near, keysT[rows, a, :, 0:P], start=True, stop=True)
                nc.tensor.matmul(s0[:, T:T + NC0], near, kcT[rows, a, 0:NC0], start=True, stop=True)
                nc.tensor.matmul(s0[:, T + 16:T + 16 + NC], far, kcT[rows, a, :], start=True, stop=True)
                nc.tensor.matmul(s1[:].rearrange("p (b k) -> p b k", b=2), far, keysT[rows, a, :, :],
                                 start=True, stop=True).then_inc(scored, 1)

            pe.wait_ge(cmp_done, 1)
            pe.wait_ge(vals_done, 2)
            scores(0)
            for e in range(HEADS + 3):
                if e + 1 < HEADS:
                    scores(e + 1)
                if 2 <= e < HEADS + 2:
                    g = e - 2
                    pe.wait_ge(normed, g + 1)
                    pe.wait_ge(normed_far, g + 1)
                    if g >= 1:
                        pe.wait_ge(probs0, g)
                    slc0, slc1, win0, win1 = (SPANS[n][0] for n in (2, 3, 4, 5))
                    for n, at in enumerate((slc0, slc1, win0, win1)):
                        mm = nc.tensor.transpose(bank[4][:, n * P:n * P + P], soft[:, g % 3, at:at + P], ident[:])
                    mm.then_inc(turned0, 1)
                    if g >= 1:
                        pe.wait_ge(probs1, g)
                    for n, at in enumerate((slc1, win1)):
                        nc.tensor.transpose(bank[5][:, n * P:n * P + P], soft[:, g % 3, at + P:at + T], ident[:])
                    if g == 0:
                        pe.wait_ge(zeroed, 1)
                    for n in range(2):
                        at = SPANS[n][0]
                        mm = nc.tensor.transpose(bank[5][0:NC, T + n * P:T + n * P + P], soft[:, g % 3, at:at + NC], ident[:])
                    mm.then_inc(turned1, 1)
                if e >= 3:
                    g = e - 3
                    i, p = g // 2, g % 2
                    grp = head_of(g) // HPG
                    pt = probsT[:, g % 2, :]
                    pe.wait_ge(probs0, g + 1)
                    pe.wait_ge(probs1, g + 1)
                    if p == 0 and i >= 1:
                        pe.wait_ge(o_lo_done, i)
                    dst = bank[6][HD * p:HD * p + HD, 0:T]
                    slc, win = (vals[:, :, n * T + HD * grp:n * T + HD * grp + HD] for n in range(2))
                    nc.tensor.matmul(dst, slc[:, 0], pt[:, 0:T], start=True, stop=False, skip_group_check=True)
                    nc.tensor.matmul(dst, win[:, 0], pt[:, T:2 * T], start=False, stop=False, skip_group_check=True)
                    nc.tensor.matmul(dst[:, P:T], slc[:, 1], pt[:, 512:640], start=False, stop=False, skip_group_check=True)
                    nc.tensor.matmul(dst[:, P:T], win[:, 1], pt[:, 640:768], start=False, stop=False, skip_group_check=True)
                    nc.tensor.matmul(dst, vc[:, HD * grp:HD * grp + HD], pt[0:NC, 768:1024], start=False, stop=True,
                                     skip_group_check=True).then_inc(headed, 1)
                if e in Q_ROUND:
                    queries(Q_ROUND[e])

            pe.wait_ge(o_lo_done, 8)
            for i in range(8):
                q = piece_of("b", "up", O_FIRST + i, 0)
                pe.wait_ge(lo_up, q["n"] + 1)
                share(i == 0, i == 7, q["slot"], gx_hi[:, i, :], gx_lo[:, i, :]).then_inc(used_up, 1)
            stage("f1")
            norm("end")


SPANS = [(0, NC0), (16, NC), (32, P), (32 + P, T), (32 + P + T, P), (32 + 2 * P + T, T)]
NARROW, WIDE = (0, 1, 2, 4), (3, 5)


def head_of(e):
    i, p = e // 2, e % 2
    return (2 * (i // HPG) + p) * HPG + i % HPG


def backwards(ap):
    return ap.rearrange("p (k t) -> p k t", k=2)[:, :, ::-1]


def UPS(st, k, i=0):
    return [(st, "up", k, c, i) for c in range(3 if st == "a" else 2)]


def B_PIECES(a, b):
    return [("b", "up", k, 0) for k in range(a, b)]


def AHEAD_A(k, i=0):
    up = UPS("a", k + 2, i)
    return up[:1], up[1:], [("a", "down", k + 1, 0, i)]


def AHEAD_F(st, k, i=0):
    up = UPS(st, k + 2, i)
    return up[:1], up[1:], [(st, "down", k + 1, 0, i)]


START_A = UPS("a", 0)[1:] + UPS("a", 1) + [("a", "down", 0, 0)]
WHILE_O = B_PIECES(NB - 2, NB) + UPS("f1", 0) + UPS("f1", 1)


def kernel(x, mix_norm, a_w_in, a_conv, a_w_out, ffn_norm, ffn_up, ffn_conv, ffn_down, kv_norm, w_kv, cmp_pe,
           cmp_w1, cmp_b1, cmp_w2, b_w_qg, b_w_o, rel_bias, final_norm):
    import concourse.bacc as bacc
    from concourse.bass_utils import run_bass_kernel_spmd as run

    c = lambda a: np.ascontiguousarray(np.asarray(a))
    tiles = lambda w, n: c(np.asarray(w).reshape(KT, P, n, P).transpose(2, 1, 0, 3)).reshape(n, P, PW)
    feat = lambda v: np.asarray(v).reshape(-1, P).T
    hd = HEADS * HD
    gains = np.concatenate([feat(v) for v in (mix_norm[0], ffn_norm[0], kv_norm, mix_norm[1], ffn_norm[1], final_norm)], 1)
    a_taps = np.asarray(a_conv)[0].reshape(3, AU, P).transpose(2, 1, 0).reshape(P, -1)
    f_taps = np.asarray(ffn_conv).reshape(2, 3, 2 * FU, P).transpose(3, 0, 2, 1).reshape(P, -1)
    pe = np.asarray(cmp_pe).reshape(2, 16, P).transpose(2, 0, 1).reshape(P, -1)
    w2 = np.asarray(cmp_w2).transpose(1, 0, 2).reshape(P, -1)
    par = np.concatenate([gains, a_taps, f_taps, pe, np.asarray(cmp_b1).T, w2], 1)
    a_up = tiles(np.asarray(a_w_in)[0], 3 * AU).reshape(3, AU, P, PW).transpose(1, 0, 2, 3)
    f_up = np.stack([tiles(w, 2 * FU).reshape(2, FU, P, PW).transpose(1, 0, 2, 3) for w in np.asarray(ffn_up)])
    kv = np.asarray(w_kv).reshape(D, 6, GROUPS * HD)
    kv_tiles = lambda s: list(tiles(kv[:, s], 2))
    val = np.concatenate([kv[:, 3], kv[:, 5]], 1).reshape(4, 2, P, 512).transpose(0, 2, 1, 3).reshape(4, P, PW)
    w1 = np.asarray(cmp_w1).reshape(2, 2, 8, P, P).transpose(0, 1, 3, 2, 4).reshape(4, P, PW)
    qg = np.asarray(b_w_qg)[0]
    heads = [head_of(e) for e in range(HEADS)]
    q = tiles(qg[:, :hd].reshape(D, HEADS, HD)[:, heads].reshape(D, hd), 8)
    g = np.zeros((P, PW), qg.dtype)
    g[:, :8 * 3 * HEADS] = qg[:, hd:].reshape(KT, P, 3 * HEADS).transpose(1, 0, 2).reshape(P, -1)
    sets = {"cmp": kv_tiles(0) + kv_tiles(1), "key": kv_tiles(2) + kv_tiles(4), "val": list(val), "w1": list(w1),
            "gate": [g], "q": list(q)}
    b_up = np.stack([sets[what][t] for what, t in B_ORDER[:O_FIRST]])
    b_down = np.asarray(b_w_o)[0].reshape(HEADS, HD, D)[heads].reshape(8, P, PW)
    arrays = {
        "xT": np.asarray(x)[0].T.reshape(KT, P, T).transpose(1, 0, 2), "par": par, "hot": one_hot_of_distances(),
        "rel": rel_bias, "a_up": a_up, "a_down": np.asarray(a_w_out)[0].reshape(AU, P, PW), "f_up": f_up,
        "f_down": np.asarray(ffn_down).reshape(2, FU, P, PW), "b_up": b_up, "b_down": b_down,
    }
    arrays = {k: c(v) for k, v in arrays.items()}
    nc = bacc.Bacc("TRN2", target_bir_lowering=False, num_devices=1)
    args = [nc.dram_tensor(f"in_{k}", v.shape, F32, kind="ExternalInput").ap() for k, v in arrays.items()]
    scratch = nc.dram_tensor("bias_rows", [HEADS, 384], F32, kind="Internal").ap()
    out = nc.dram_tensor("out", (P, KT, T), F32, kind="ExternalOutput").ap()
    build(nc, *args, scratch, out)
    r = run(nc, [{f"in_{k}": v for k, v in arrays.items()}], core_ids=[0])
    return c(r.results[0]["out"].transpose(2, 1, 0)).reshape(1, T, D)
```

```python
import math
from contextlib import ExitStack

import numpy as np

import concourse.bass as bass
from concourse import mybir

ALU = mybir.AluOpType
ACT = mybir.ActivationFunctionType
F32 = mybir.dt.float32
F32R = mybir.dt.float32r

P = 128
D = 1024
T = 256
KT = D // P
F = 2816
FU = F // P
AU = D // P
HEADS = 16
GROUPS = 4
HPG = HEADS // GROUPS
HD = 64
CL, CS = 32, 16
NC = (T - CL) // CS + 1
BUCKETS = 32
MAXD = 128
EPS = 1e-6
NEG = -1e30
PW = 1024

PAR = {}
_at = 0
for _name, _n in (("gains", 6 * KT), ("a_taps", 3 * AU), ("f_taps", 2 * 2 * FU * 3), ("pe", 2 * 16),
                  ("b1", 2), ("w2", 2 * HD)):
    PAR[_name] = _at
    _at += _n
NPAR = _at
GAIN = {"mix0": 0, "ffn0": 1, "kv": 2, "mix1": 3, "ffn1": 4, "final": 5}

B_ORDER = ([("cmp", t) for t in range(4)] + [("key", t) for t in range(4)] + [("val", t) for t in range(4)]
           + [("w1", 0), ("gate", 0), ("w1", 1), ("q", 0), ("w1", 2), ("q", 1), ("w1", 3)] + [("q", t) for t in range(2, 8)]
           + [("o", t) for t in range(8)])
NB = len(B_ORDER)
UP_SLOTS, DOWN_SLOTS = 6, 3
AHEAD = UP_SLOTS
WARM = 18
O_FIRST = B_ORDER.index(("o", 0))
Q_BEFORE = 5
Q_ROUND = {1: 5, 2: 6, 6: 7}
O_ROUND = {HEADS - 1: (0,), HEADS: (1,), HEADS + 1: (2, 3)}


def q_index(t):
    return B_ORDER.index(("q", t))


NC0 = (P - CL) // CS + 1


def plan_pieces():
    order = [("a", "up", u, c) for u in range(AU) for c in range(3)]
    order += [("f0", "up", u, c) for u in range(FU) for c in range(2)]
    order += [("b", "up", b, 0) for b in range(NB)]
    order += [("f1", "up", u, c) for u in range(FU) for c in range(2)]
    downs = [("a", "down", u, 0) for u in range(AU)] + [("f0", "down", u, 0) for u in range(FU)]
    downs += [("f1", "down", u, 0) for u in range(FU)]
    table = {}
    for keys in (order, downs):
        used, turns = {}, {}
        for n, key in enumerate(keys):
            st, kind, u, c = key
            if kind == "up":
                slot = {"a": 3 * (u % 2) + c, "b": (u + 2) % 6}.get(st, 2 * (u % 3) + c)
            else:
                slot = UP_SLOTS + (u % 3 if st != "a" else {AU - 2: 2, AU - 1: 0}.get(u, u % 2))
            turns[slot] = turns.get(slot, 0) + 1
            table[key] = dict(n=n, slot=slot, turn=turns[slot], prev=used.get(slot))
            used[slot] = n
    return table


def bucket_of(dist):
    half = BUCKETS // 2
    if dist < half:
        return dist
    large = half + int(np.float32(np.log(np.float32(dist) / np.float32(half))) / np.float32(math.log(MAXD / half))
                       * np.float32(BUCKETS - half))
    return min(large, BUCKETS - 1)


def one_hot_of_distances():
    hot = np.zeros((BUCKETS + 1, 512), np.float32)
    for m in range(511):
        hot[bucket_of(255 - m) if m <= 255 else BUCKETS, m] = 1.0
    return hot


def build(nc, xT, par, hot, rel, a_up, a_down, f_up, f_down, b_up, b_down, scratch, out):
    piece = plan_pieces()
    ctx = ExitStack()
    with ctx:
        def sb(name, shape, dt=F32):
            return ctx.enter_context(nc.sbuf_tensor(name, shape, dt))

        def sem(name):
            return ctx.enter_context(nc.semaphore(name))

        x = sb("x", [P, KT, T])
        gx = sb("gx", [P, 2, KT * T], F32R)
        gx_hi, gx_lo = (gx[:, n, :].rearrange("p (k t) -> p k t", k=KT) for n in range(2))
        gq_hi = sb("gq_hi", [P, KT, T], F32R)
        gq_lo = sb("gq_lo", [P, KT, T], F32R)
        w_hi = sb("w_hi", [P, UP_SLOTS + DOWN_SLOTS, PW], F32R)
        w_lo = sb("w_lo", [P, UP_SLOTS + DOWN_SLOTS, PW], F32R)
        staged = sb("staged", [P, UP_SLOTS + 1, PW])
        bias = sb("bias", [P, HEADS, T])
        y = sb("y", [P, 2, 16 * 4 * NC], F32R)
        y_hi, y_lo = y[:, 0, :], y[:, 1, :]
        params = sb("params", [P, NPAR])
        rstd = sb("rstd", [P, T])
        sumsq = sb("sumsq", [P, 2, T])
        ones = sb("ones", [P, P])
        ident = sb("ident", [P, P])
        eps = sb("eps", [P, 1])
        vc = sb("vc", [NC, GROUPS * HD])
        WORK = 8576
        work = sb("work", [P, WORK])

        def part(at, n, rows=P):
            return work[0:rows, at:at + n]

        shifted = part(0, 3 * 2 * 258).rearrange("p (r c t) -> p r c t", r=3, c=2)
        conv = part(1548, 3 * 2 * T).rearrange("p (r c t) -> p r c t", r=3, c=2)
        squares = part(3084, 1024).rearrange("p (b n) -> p b n", b=2)
        deviation = part(4108, T)
        squares_end = [part(3084 + 512 * b, 512) for b in range(4)]
        hot_sb = part(4400, 512, BUCKETS + 1)
        table_sb = part(5424, HEADS, BUCKETS + 1)
        rows_sb = part(5440, 384, HEADS)
        rstd2 = part(5840, T)
        tokens = part(0, 2048).rearrange("p (j g t) -> p j g t", j=2, g=GROUPS)
        block_in = part(2048, 16 * 4 * NC)
        gelu = part(3008, 5 * 120).rearrange("p (k n) -> p k n", k=5)
        gateT = part(3616, T, 3 * HEADS)
        NS = 800
        soft = part(0, 3 * NS).rearrange("p (r n) -> p r n", r=3)
        probsT = part(3 * NS, 2 * 1024).rearrange("p (r n) -> p r n", r=2)
        Q0 = 3 * NS + 2048
        qT = part(Q0, 8 * T).rearrange("p (i t) -> p i t", i=8)
        keysT = part(Q0 + 2048, 2 * (NC + 2 * T)).rearrange("p (a n) -> p a n", a=2)
        vals = part(Q0 + 2048 + 2 * (NC + 2 * T), 2 * 512).rearrange("p (k n) -> p k n", k=2)
        assert Q0 + 3072 + 2 * (NC + 2 * T) <= WORK
        stats = sb("stats", [P, 3, 18])
        gate = sb("gate", [P, 2, 3 * HEADS])
        rowmask = sb("rowmask", [P, 1])
        rstd_t = sb("rstd_t", [P, 4])
        tiny = sb("tiny", [P, 12])

        bank = [ctx.enter_context(nc.psum_tensor(f"bank{i}", [P, 512], F32)) for i in range(8)]

        landed = [sem(f"landed{s}") for s in range(UP_SLOTS + 1)]
        x_landed = [sem(f"x_landed{b}") for b in range(4)]
        par_landed, hot_landed, bias_landed = sem("par_landed"), sem("hot_landed"), sem("bias_landed")
        hi_up, lo_up, used_up = sem("hi_up"), sem("lo_up"), sem("used_up")
        hi_down, lo_down, used_down = sem("hi_down"), sem("lo_down"), sem("used_down")
        scaled, tapped, convolved, silued, y_done, y_hi_done, y_lo_done = (
            {s: sem(f"{n}_{s}") for s in ("a", "f0", "f1")}
            for n in ("scaled", "tapped", "convolved", "silued", "y_done", "y_hi_done", "y_lo_done"))
        acc_done, x_new = sem("acc_done"), sem("x_new")
        gx_hi_done, gx_lo_done = sem("gx_hi_done"), sem("gx_lo_done")
        gq_hi_done, gq_lo_done = sem("gq_hi_done"), sem("gq_lo_done")
        squared, summed, norm_summed = sem("squared"), sem("summed"), sem("norm_summed")
        deviated, rstd_done, padded = sem("deviated"), sem("rstd_done"), sem("padded")
        consts_done, table_done, rows_done, rows_copied = sem("consts_done"), sem("table_done"), sem("rows_done"), sem("rows_copied")
        rows_stored = sem("rows_stored")
        b_evacuated, tokens_shifted, block_done = sem("b_evacuated"), sem("tokens_shifted"), sem("block_done")
        block_hi_done, block_lo_done = sem("block_hi_done"), sem("block_lo_done")
        vals_done, gate_read, gate_exp, gate_turned, gate_step, gate_done = (
            sem("vals_done"), sem("gate_read"), sem("gate_exp"), sem("gate_turned"), sem("gate_step"), sem("gate_done"))
        pre_gelu, gelu_step, gelu_tanh, hidden_done = sem("pre_gelu"), sem("gelu_step"), sem("gelu_tanh"), sem("hidden_done")
        cmp_mm, cmp_done = sem("cmp_mm"), sem("cmp_done")
        scored, biased, exped = sem("scored"), sem("biased"), sem("exped")
        recipd, weighted, normed, normed_far = sem("recipd"), sem("weighted"), sem("normed"), sem("normed_far")
        turned0, turned1, probs0, probs1 = sem("turned0"), sem("turned1"), sem("probs0"), sem("probs1")
        headed, o_hi_done, o_lo_done = sem("headed"), sem("o_hi_done"), sem("o_lo_done")
        zeroed = sem("zeroed")
        x_gained, x_far_gained = sem("x_gained"), sem("x_far_gained")
        out_done, out_far_done, stored = sem("out_done"), sem("out_far_done"), sem("stored")

        NORM = {"a": 0, "f0": 1, "b": 2, "f1": 3, "end": 4}
        GAIN_OF = {"a": "mix0", "f0": "ffn0", "b": "kv", "f1": "ffn1"}
        LAST_PIECE = {"f0": (used_down, piece[("a", "down", AU - 1, 0)]["n"]), "b": (used_down, piece[("f0", "down", FU - 1, 0)]["n"]),
                      "f1": (used_up, piece[("b", "up", NB - 1, 0)]["n"]), "end": (used_down, piece[("f1", "down", FU - 1, 0)]["n"])}
        RSTD_AT = {"a": 2, "f0": 3, "b": 5, "f1": 6, "end": 7}

        def looped(i):
            return not isinstance(i, int)

        ROUNDS = 6

        def gain(name, kt):
            at = PAR["gains"] + GAIN[name] * KT + kt
            return params[:, at:at + 1]

        def tap(st, c, i, k, ring, which):
            if st == "a":
                at = PAR["a_taps"] + 3 * k + which + 3 * ring * i
            else:
                at = PAR["f_taps"] + 3 * ((int(st[1]) * 2 + c) * FU + k) + which + 3 * ring * i
            return params[:, bass.ds(at, 1)]

        def gains_end(eng, queue, tiles, done):
            for kt in tiles:
                queue.wait_ge(squared, 4 * NORM["end"] + kt // 2 + 1)
                eng.tensor_scalar(x[:, kt, :], x[:, kt, :], gain("final", kt), None, ALU.mult).then_inc(done, 1)

        def piece_of(st, kind, k, c):
            return piece[(st, kind, k, c)]

        def before(q, st, kind):
            if st[0] == "f" and kind == "down":
                return max(-1 if q["prev"] is None else q["prev"], q["n"] - DOWN_SLOTS)
            return q["prev"]

        def stride(st, kind):
            return {"a": {"up": 6, "down": 2}}.get(st, {"up": 6, "down": 3})[kind]

        blocks = [y[:], gx[:, :, 0:16 * 4 * NC]]
        hidden = [bank[6], bank[3]]

        def pair_bank(b):
            return bank[b // 2 % 3][:, b % 2 * T:(b % 2 + 1) * T]

        ACC = {"a": 4, "f0": 4, "b": 0, "f1": 0}
        UP = {"a": 0, "f0": 0, "f1": 4}
        NORM_BANK = {"a": 3, "f0": 3, "b": 3, "f1": 7, "end": 7}
        ACC_BEFORE = {"f0": ACC["a"], "b": ACC["f0"], "f1": ACC["b"], "end": ACC["f1"]}

        def q_bank(t):
            return bank[{0: 1, 1: 0, 2: 2}.get(t, 7)][:, 0:T]

        block = ctx.enter_context(nc.Block())

        @block.sync
        def _(sp):
            def load(st, kind, k, c, i=0):
                q = piece_of(st, kind, k, c)
                move = stride(st, kind) * i
                ring = 2 if st == "a" else 3
                s = min(q["slot"], UP_SLOTS)
                if kind == "up":
                    if q["prev"] is not None:
                        sp.wait_ge(lo_up, q["prev"] + 1 + move)
                elif q["n"] > 0 or looped(i):
                    sp.wait_ge(lo_down, q["n"] + move)
                unit = k + ring * i
                if st == "a":
                    src = a_up[unit, c] if kind == "up" else a_down[unit]
                elif st == "b":
                    src = b_up[k] if k < O_FIRST else b_down[k - O_FIRST]
                else:
                    src = f_up[int(st[1]), unit, c] if kind == "up" else f_down[int(st[1]), unit]
                n = 8 * 3 * HEADS if st == "b" and B_ORDER[k][0] == "gate" else PW
                sp.dma_start(staged[:, s, 0:n], src[:, 0:n]).then_inc(landed[s], 16)

            def ups(st, k, i=0):
                for c in range(3 if st == "a" else 2):
                    load(st, "up", k, c, i)

            def b_pieces(first, last):
                for b in range(first, last):
                    load("b", "up", b, 0)

            def x_tiles(b):
                sp.dma_start(x[:, 2 * b:2 * b + 2, :], xT[:, 2 * b:2 * b + 2, :]).then_inc(x_landed[b], 16)

            x_tiles(0)
            sp.dma_start(params[:], par).then_inc(par_landed, 16)
            x_tiles(1)
            load("a", "up", 0, 0)
            x_tiles(2)
            x_tiles(3)
            load("a", "up", 0, 1)
            load("a", "up", 0, 2)
            sp.dma_start(hot_sb, hot).then_inc(hot_landed, 16)
            sp.dma_start(table_sb[0:BUCKETS, :], rel).then_inc(hot_landed, 16)
            ups("a", 1)
            for k in (2, 3):
                ups("a", k)
                load("a", "down", k - 2, 0)
            with sp.Fori(1, AU // 2 - 1) as i:
                for k in (2, 3):
                    ups("a", k, i)
                    load("a", "down", k - 2, 0, i)
            ups("f0", 0)
            load("a", "down", AU - 2, 0)
            ups("f0", 1)
            load("a", "down", AU - 1, 0)
            for st in ("f0", "f1"):
                load(st, "down", 0, 0)
                ups(st, 2)
                load(st, "down", 1, 0)
                with sp.Fori(0, ROUNDS) as i:
                    for k in (3, 4, 5):
                        ups(st, k, i)
                        load(st, "down", k - 1, 0, i)
                ups(st, FU - 1)
                if st == "f0":
                    b_pieces(0, 4)
                load(st, "down", FU - 2, 0)
                if st == "f0":
                    b_pieces(4, 6)
                load(st, "down", FU - 1, 0)
                if st == "f0":
                    b_pieces(6, NB)
                    ups("f1", 0)
                    ups("f1", 1)
            for b in range(4):
                sp.wait_ge(*((out_done, b + 1) if b < 3 else (out_far_done, 1)))
                sp.dma_start(out[:, 2 * b:2 * b + 2, :], x[:, 2 * b:2 * b + 2, :]).then_inc(stored, 16)
            sp.wait_ge(stored, 64)

        @block.gpsimd
        def _(pool):
            nc.gpsimd.memset(ones[:], 1.0).then_inc(consts_done, 1)
            nc.gpsimd.memset(ident[:], 0.0).then_inc(consts_done, 1)
            nc.gpsimd.memset(eps[:], EPS).then_inc(consts_done, 1)
            nc.gpsimd.memset(rowmask[:], 1.0).then_inc(consts_done, 1)
            pool.wait_ge(consts_done, 4)
            nc.gpsimd.affine_select(out=ident[:], in_=ident[:], compare_op=ALU.not_equal, fill=1.0, base=0,
                                    pattern=[[-1, P]], channel_multiplier=1).then_inc(consts_done, 1)
            nc.gpsimd.affine_select(out=rowmask[:], in_=rowmask[:], compare_op=ALU.is_ge, fill=0.0, base=P - CL,
                                    pattern=[[0, 1]], channel_multiplier=-1).then_inc(consts_done, 1)

            def norm(st):
                k = NORM[st]
                for b in range(1, 3):
                    pool.wait_ge(squared, 4 * k + b + 1)
                    if b > 1:
                        pool.wait_ge(summed, 2 * k + 1)
                    total = sumsq[:].rearrange("p h t -> p (h t)")
                    nc.gpsimd.tensor_tensor(total, total, squares[:, b % 2, :], ALU.add).then_inc(summed, 1)

            def pads(n):
                nc.gpsimd.memset(shifted[:, :, :, 0:2], 0.0).then_inc(padded, 1)

            def rest(st, kind, k, c):
                q = piece_of(st, kind, k, c)
                hi, lo = (hi_up, lo_up) if kind == "up" else (hi_down, lo_down)
                pool.wait_ge(hi, q["n"] + 1)
                pool.wait_ge(lo, q["n"])
                nc.gpsimd.tensor_tensor(w_lo[:, q["slot"], :], staged[:, min(q["slot"], UP_SLOTS), :],
                                        w_hi[:, q["slot"], :].bitcast(F32), ALU.subtract).then_inc(lo, 1)

            pads(0)
            norm("a")
            pool.wait_ge(rows_copied, 1)
            pool.dma_start(scratch, rows_sb).then_inc(rows_stored, 16)
            pool.wait_ge(rows_stored, 16)
            diagonals = bass.AP(tensor=scratch.tensor, offset=0, ap=[[1, P], [384, HEADS], [1, T]])
            pool.dma_start(bias[:], diagonals).then_inc(bias_landed, 16)
            rest("a", "down", AU - 1, 0)
            rest("f0", "up", 1, 1)
            norm("f0")
            rest("f0", "down", FU - 1, 0)
            rest("b", "up", 3, 0)
            norm("b")
            for j in range(2):
                pool.wait_ge(tokens_shifted, j + 1)
                if j:
                    pool.wait_ge(block_lo_done, 1)
                tok, pe_j = tokens[:, j, 0, 0:1], params[:, PAR["pe"] + 16 * j:PAR["pe"] + 16 * j + 16]
                tok = bass.AP(tensor=tok.tensor, offset=tok.offset, ap=[tok.ap[0], [2, 16], [T, GROUPS], [CS, NC]])
                pe_j = pe_j.unsqueeze(2).unsqueeze(3).to_broadcast([P, 16, GROUPS, NC])
                nc.gpsimd.tensor_tensor(block_in.rearrange("p (i g c) -> p i g c", i=16, g=GROUPS), tok, pe_j,
                                        ALU.add).then_inc(block_done, 1)
                pool.wait_ge(block_hi_done, j + 1)
                nc.gpsimd.tensor_tensor(blocks[j][:, 1, :], block_in, blocks[j][:, 0, :].bitcast(F32),
                                        ALU.subtract).then_inc(block_lo_done, 1)
            pool.wait_ge(block_lo_done, 2)
            nc.gpsimd.memset(soft[:, :, NC0:NC], 0.0).then_inc(zeroed, 1)
            for e in range(HEADS):
                pool.wait_ge(weighted, e + 1)
                for n in NARROW:
                    at, w = SPANS[n]
                    q = nc.gpsimd.tensor_scalar(soft[:, e % 3, at:at + w], soft[:, e % 3, at:at + w],
                                                stats[:, e % 3, 12 + n:13 + n], None, ALU.mult)
                q.then_inc(normed, 1)
            pool.wait_ge(headed, HEADS)
            pads(1)
            rest("f1", "up", 1, 1)
            norm("f1")
            rest("f1", "down", FU - 1, 0)
            gains_end(nc.gpsimd, pool, range(KT - 2, KT), x_far_gained)
            pool.wait_ge(x_far_gained, 2)
            pool.wait_ge(rstd_done, RSTD_AT["end"])
            nc.gpsimd.tensor_tensor(x[:, 6:8, :], x[:, 6:8, :], rstd[:].unsqueeze(1).to_broadcast([P, 2, T]),
                                    ALU.mult).then_inc(out_far_done, 1)

        @block.scalar
        def _(act):
            preloads = []

            def preload(func):
                n = len(preloads)
                preloads.append(func)
                nc.scalar.activation(tiny[:, n:n + 1], eps[:], func)

            act.wait_ge(consts_done, 3)
            preload(ACT.Copy)

            def lead(st, kind, k, c, i=0):
                q = piece_of(st, kind, k, c)
                move = stride(st, kind) * i
                s = min(q["slot"], UP_SLOTS)
                hi, used = (hi_up, used_up) if kind == "up" else (hi_down, used_down)
                if kind == "up":
                    act.wait_ge(landed[s], 16 * q["turn"] + 16 * i)
                else:
                    act.wait_ge(landed[s], 16 * (q["n"] + 1) + 16 * move)
                last = before(q, st, kind)
                if last is not None and last >= 0:
                    act.wait_ge(used, last + 1 + move)
                n = 8 * 3 * HEADS if st == "b" and B_ORDER[k][0] == "gate" else PW
                nc.scalar.activation(w_hi[:, q["slot"], 0:n], staged[:, s, 0:n], ACT.Copy).then_inc(hi, 1)

            def norm(st, between=(), meanwhile=()):
                k = NORM[st]

                def leads(b):
                    for kt in (2 * b, 2 * b + 1):
                        nc.scalar.activation(gx_hi[:, kt, :], x[:, kt, :], ACT.Copy,
                                             scale=gain(GAIN_OF[st], kt)).then_inc(gx_hi_done, 1)

                if st == "a":
                    act.wait_ge(par_landed, 16)
                    for b in range(4):
                        act.wait_ge(x_landed[b], 16)
                        leads(b)
                        if b == 1:
                            lead("a", "up", 0, 0)
                    for q in between:
                        lead(*q)
                if st == "end":
                    preload(ACT.Sqrt)
                for b in range(4):
                    if st != "a":
                        act.wait_ge(x_new, 4 * (k - 1) + b + 1)
                    if st not in ("a", "end"):
                        leads(b)
                    if st == "end":
                        dst = squares_end[b]
                    elif b == 0:
                        dst = sumsq[:].rearrange("p h t -> p (h t)")
                    else:
                        if b == 3:
                            act.wait_ge(summed, 2 * k + 1)
                        dst = squares[:, b % 2, :]
                    nc.scalar.activation(dst, x[:, 2 * b:2 * b + 2, :].rearrange("p k t -> p (k t)"),
                                         ACT.Square).then_inc(squared, 1)
                if st != "end":
                    preload(ACT.Sqrt)
                for q in meanwhile:
                    lead(*q)
                act.wait_ge(norm_summed, k + 1)
                q = nc.scalar.activation(deviation, bank[NORM_BANK[st]][:, 0:T], ACT.Sqrt, bias=eps[:], scale=1.0 / D)
                if st == "b":
                    q = nc.scalar.activation(rstd_t[:, 2:4], bank[NORM_BANK[st]][:, T:T + 2], ACT.Sqrt, bias=eps[:], scale=1.0 / D)
                q.then_inc(deviated, 1)
                if st[0] == "f":
                    preload(ACT.Silu)

            def step(st, k, ahead, i=0):
                ring = 2 if st == "a" else 3
                r = k % ring
                u = k + ring * i
                early, middle, late = ahead
                for q in early:
                    lead(*q)
                for c in range(1 if st == "a" else 2):
                    if c == 0:
                        act.wait_ge(scaled[st], u + 1)
                    nc.scalar.activation(conv[:, r, c, :], shifted[:, r, c, 2:2 + T], ACT.Copy,
                                         scale=tap(st, c, i, k, ring, 2)).then_inc(tapped[st], 1)
                for q in middle:
                    lead(*q)
                if st != "a":
                    act.wait_ge(convolved[st], 4 * u + 3)
                    nc.scalar.activation(conv[:, r, 0, :], conv[:, r, 0, :], ACT.Silu).then_inc(silued[st], 1)
                act.wait_ge(y_done[st], u + 1)
                q = piece_of(st, "down", k, 0)
                back = {"a": 2, "f0": 3, "f1": 3}[st]
                if k >= back or looped(i):
                    act.wait_ge(used_down, q["n"] - back + 1 + stride(st, "down") * i)
                nc.scalar.activation(y_hi[:, r * T:(r + 1) * T], conv[:, r, 1, :], ACT.Copy).then_inc(y_hi_done[st], 1)
                for q in late:
                    lead(*q)

            def stage(st, nxt):
                if st == "a":
                    step(st, 0, AHEAD_A(0))
                    step(st, 1, AHEAD_A(1))
                    with act.Fori(0, 2) as i:
                        for k in (2, 3):
                            step(st, k, AHEAD_A(k, i), i)
                    step(st, AU - 2, ([("a", "down", AU - 2, 0)] + nxt[0:1], nxt[1:2], nxt[2:3] + [("a", "down", AU - 1, 0)]))
                    step(st, AU - 1, ([], [], nxt[3:]))
                else:
                    step(st, 0, ([], [], [(st, "down", 1, 0)]))
                    with act.Fori(0, ROUNDS) as i:
                        for k in (1, 2, 3):
                            step(st, k, AHEAD_F(st, k, i), i)
                    early, middle, late = AHEAD_F(st, FU - 3)
                    step(st, FU - 3, (early, middle, late + nxt[0:1]))
                    step(st, FU - 2, (nxt[1:2], nxt[2:3], [(st, "down", FU - 1, 0)]))
                    step(st, FU - 1, ([], [], nxt[3:]))

            norm("a", between=UPS("a", 0)[1:], meanwhile=UPS("a", 1))
            stage("a", UPS("f0", 0) + UPS("f0", 1))
            norm("f0", meanwhile=SOON("f0"))
            stage("f0", B_PIECES(0, 4))
            norm("b", meanwhile=B_PIECES(4, 6))
            for kt in range(KT):
                nc.scalar.activation(gq_hi[:, kt, :], x[:, kt, :], ACT.Copy, scale=gain("mix1", kt)).then_inc(gq_hi_done, 1)

            UB = piece[("b", "up", 0, 0)]["n"]
            for b, (what, t) in enumerate(B_ORDER):
                if b in (2, 4):
                    j = b // 2 - 1
                    act.wait_ge(b_evacuated, 2 * j + 2)
                    nc.scalar.activation(tokens[HD:P, j, :, 0:T - 1], tokens[0:HD, j, :, 1:T], ACT.Copy).then_inc(tokens_shifted, 1)
                if b in (6, 12):
                    j = 0 if b == 6 else 1
                    act.wait_ge(block_done, j + 1)
                    if j:
                        act.wait_ge(used_up, UB + B_ORDER.index(("val", 3)) + 1)
                    nc.scalar.activation(blocks[j][:, 0, :], block_in, ACT.Copy).then_inc(block_hi_done, 1)
                if what == "val" and t == 3:
                    act.wait_ge(used_up, UB + b + 1)
                    act.wait_ge(rstd_done, RSTD_AT["b"])
                    for k in range(2):
                        nc.scalar.activation(vals[:, k, :], bank[4 + k][:], ACT.Copy, scale=rstd_t[:, k:k + 1]).then_inc(vals_done, 1)
                if what == "gate":
                    act.wait_ge(gate_read, 1)
                    nc.scalar.activation(gateT, gateT, ACT.Exp).then_inc(gate_exp, 1)
                if (what, t) == ("q", 2):
                    act.wait_ge(gelu_step, 3)
                    nc.scalar.activation(gelu[:, 3, :], gelu[:, 2, :], ACT.Tanh, scale=math.sqrt(2 / math.pi)).then_inc(gelu_tanh, 1)
                lead("b", "up", b + AHEAD, 0)
                if (what, t) == ("q", Q_BEFORE - 1):
                    break

            for e in range(HEADS + 4):
                if e >= 5 and e % 2 == 1:
                    i = (e - 5) // 2
                    act.wait_ge(headed, 2 * i + 2)
                    nc.scalar.activation(gx_hi[:, i, :].rearrange("p (k t) -> p k t", k=2), backwards(bank[6][:, 0:T]),
                                         ACT.Copy).then_inc(o_hi_done, 1)
                if e < HEADS:
                    act.wait_ge(biased, e + 1)
                    if e >= 3:
                        act.wait_ge(recipd, e - 2)
                    for n, (at, w) in enumerate(SPANS):
                        q = nc.scalar.activation(soft[:, e % 3, at:at + w], soft[:, e % 3, at:at + w], ACT.Exp, scale=-1.0,
                                                 bias=stats[:, e % 3, n:n + 1], accum_out=stats[:, e % 3, 6 + n:7 + n])
                    q.then_inc(exped, 1)
                if 2 <= e < HEADS + 2:
                    h = e - 2
                    act.wait_ge(turned0, h + 1)
                    if h >= 2:
                        act.wait_ge(headed, h - 1)
                    nc.scalar.activation(probsT[:, h % 2, 0:512], bank[4][:], ACT.Copy).then_inc(probs0, 1)
                if e in Q_ROUND:
                    lead("b", "up", q_index(Q_ROUND[e]) + AHEAD, 0)
            for q in WHILE_O:
                lead(*q)
            norm("f1", meanwhile=SOON("f1"))
            stage("f1", [])
            norm("end")

        @block.vector
        def _(dve):
            def rest(st, kind, k, c, i=0):
                q = piece_of(st, kind, k, c)
                move = stride(st, kind) * i
                s = min(q["slot"], UP_SLOTS)
                hi, lo = (hi_up, lo_up) if kind == "up" else (hi_down, lo_down)
                dve.wait_ge(hi, q["n"] + 1 + move)
                if (st, kind, k, c) in AFTER_POOL and not looped(i):
                    dve.wait_ge(lo, q["n"])
                n = 8 * 3 * HEADS if st == "b" and B_ORDER[k][0] == "gate" else PW
                nc.vector.tensor_tensor(w_lo[:, q["slot"], 0:n], staged[:, s, 0:n], w_hi[:, q["slot"], 0:n].bitcast(F32),
                                        ALU.subtract).then_inc(lo, 1)

            def norm(st, between=(), meanwhile=()):
                k = NORM[st]

                def residual(b):
                    if b < 3:
                        dve.wait_ge(acc_done, 3 * (k - 1) + b + 1)
                    else:
                        done, n = LAST_PIECE[st]
                        dve.wait_ge(done, n + 1)
                    xb = x[:, 2 * b:2 * b + 2, :].rearrange("p k t -> p (k t)")
                    nc.vector.tensor_tensor(xb, xb, bank[ACC_BEFORE[st] + b][:], ALU.add).then_inc(x_new, 1)

                if st != "a":
                    residual(0)
                    residual(1)
                for b in range(4):
                    if st != "end":
                        for kt in (2 * b, 2 * b + 1):
                            dve.wait_ge(gx_hi_done, 8 * k + kt + 1)
                            if st == "a":
                                dve.wait_ge(par_landed, 16)
                                dve.wait_ge(x_landed[b], 16)
                            nc.vector.scalar_tensor_tensor(gx_lo[:, kt, :], x[:, kt, :], gain(GAIN_OF[st], kt),
                                                           gx_hi[:, kt, :].bitcast(F32), ALU.mult, ALU.subtract).then_inc(gx_lo_done, 1)
                    if st == "a" and b == 1:
                        rest("a", "up", 0, 0)
                    if st != "a" and b < 2:
                        residual(b + 2)
                if st == "end":
                    gains_end(nc.vector, dve, range(KT - 2), x_gained)
                for q in (*between, *meanwhile):
                    rest(*q)
                dve.wait_ge(deviated, k + 1)
                nc.vector.reciprocal(rstd[:], deviation).then_inc(rstd_done, 1)
                if st == "a":
                    dve.wait_ge(rstd_done, 1)
                    nc.vector.tensor_tensor(rstd2, rstd[:], rstd[:], ALU.mult).then_inc(rstd_done, 1)
                elif st == "b":
                    nc.vector.reciprocal(rstd_t[:, 0:2], rstd_t[:, 2:4]).then_inc(rstd_done, 1)
                dve.wait_ge(rstd_done, RSTD_AT[st])

            def step(st, k, ahead, i=0):
                ring = 2 if st == "a" else 3
                r = k % ring
                u = k + ring * i
                early, middle, late = ahead
                last = piece_of(st, "up", k, 2 if st == "a" else 1)
                dve.wait_ge(used_up, last["n"] + 1 + stride(st, "up") * i)
                if st == "a":
                    nc.vector.tensor_tensor(shifted[:, r, 1, 2:2 + T], bank[2 * r][:, 0:T], rstd[:], ALU.mult)
                    nc.vector.tensor_tensor(conv[:, r, 1, :], bank[2 * r][:, T:2 * T], rstd2, ALU.mult).then_inc(convolved[st], 1)
                    dve.wait_ge(convolved[st], 3 * u + 1)
                    nc.vector.tensor_tensor(shifted[:, r, 0, 2:2 + T], bank[2 * r + 1][:, 0:T], conv[:, r, 1, :],
                                            ALU.mult).then_inc(scaled[st], 1)
                    halves, per, off = 1, 3, 1
                else:
                    nc.vector.tensor_tensor(shifted[:, r, :, 2:2 + T], bank[UP[st] + r][:].rearrange("p (c t) -> p c t", c=2),
                                            rstd[:].unsqueeze(1).to_broadcast([P, 2, T]), ALU.mult).then_inc(scaled[st], 1)
                    halves, per, off = 2, 4, 0
                for q in early:
                    rest(*q)
                for c in range(halves):
                    dve.wait_ge(tapped[st], halves * u + c + 1)
                    nc.vector.scalar_tensor_tensor(conv[:, r, c, :], shifted[:, r, c, 1:1 + T], tap(st, c, i, k, ring, 1),
                                                   conv[:, r, c, :], ALU.mult, ALU.add).then_inc(convolved[st], 1)
                for c in range(halves):
                    dve.wait_ge(convolved[st], per * u + off + c + 1)
                    nc.vector.scalar_tensor_tensor(conv[:, r, c, :], shifted[:, r, c, 0:T], tap(st, c, i, k, ring, 0),
                                                   conv[:, r, c, :], ALU.mult, ALU.add).then_inc(convolved[st], 1)
                for q in middle:
                    rest(*q)
                dve.wait_ge(convolved[st], per * u + per)
                if st == "a":
                    nc.vector.tensor_tensor(conv[:, r, 1, :], conv[:, r, 0, :], shifted[:, r, 1, 2:2 + T],
                                            ALU.mult).then_inc(y_done[st], 1)
                else:
                    dve.wait_ge(silued[st], u + 1)
                    nc.vector.tensor_tensor(conv[:, r, 1, :], conv[:, r, 0, :], conv[:, r, 1, :],
                                            ALU.mult).then_inc(y_done[st], 1)
                dve.wait_ge(y_hi_done[st], u + 1)
                nc.vector.tensor_tensor(y_lo[:, r * T:(r + 1) * T], conv[:, r, 1, :], y_hi[:, r * T:(r + 1) * T].bitcast(F32),
                                        ALU.subtract).then_inc(y_lo_done[st], 1)
                for q in late:
                    rest(*q)

            def stage(st, nxt):
                if st == "a":
                    step(st, 0, AHEAD_A(0))
                    step(st, 1, AHEAD_A(1))
                    with dve.Fori(0, 2) as i:
                        for k in (2, 3):
                            step(st, k, AHEAD_A(k, i), i)
                    step(st, AU - 2, ([("a", "down", AU - 2, 0)] + nxt[0:1], nxt[1:2], nxt[2:3]))
                    step(st, AU - 1, NOTHING)
                else:
                    step(st, 0, ([], [], [(st, "down", 1, 0)]))
                    with dve.Fori(0, ROUNDS) as i:
                        for k in (1, 2, 3):
                            step(st, k, AHEAD_F(st, k, i), i)
                    early, middle, late = AHEAD_F(st, FU - 3)
                    step(st, FU - 3, (early, middle, late + nxt[0:1]))
                    step(st, FU - 2, (nxt[1:2], nxt[2:3], []))
                    step(st, FU - 1, NOTHING)

            nc.vector.memset(table_sb[BUCKETS:BUCKETS + 1, :], NEG).then_inc(table_done, 1)
            norm("a", between=UPS("a", 0)[1:], meanwhile=UPS("a", 1))
            dve.wait_ge(rows_done, 1)
            nc.vector.tensor_copy(rows_sb, bank[4][0:HEADS, 0:384]).then_inc(rows_copied, 1)
            dve.wait_ge(padded, 1)
            stage("a", UPS("f0", 0) + UPS("f0", 1))
            norm("f0", meanwhile=SOON("f0"))
            stage("f0", B_PIECES(0, 4))
            norm("b", meanwhile=B_PIECES(4, 6))

            UB = piece[("b", "up", 0, 0)]["n"]

            def query(t):
                dve.wait_ge(used_up, UB + q_index(t) + 1)
                nc.vector.scalar_tensor_tensor(backwards(qT[:, t, :]), q_bank(t).rearrange("p (k t) -> p k t", k=2), HD ** -0.5,
                                               rstd[:].rearrange("p (k t) -> p k t", k=2), ALU.mult, ALU.mult).then_inc(b_evacuated, 1)

            for b, (what, t) in enumerate(B_ORDER):
                if what in ("cmp", "key"):
                    dve.wait_ge(used_up, UB + b // 2 * 2 + 2)
                    src = pair_bank(b)
                if what == "cmp":
                    j, a = t // 2, t % 2
                    for p in range(2):
                        q = nc.vector.tensor_tensor(tokens[0:HD, j, 2 * a + p, :], src[HD * p:HD * p + HD, :],
                                                    rstd[0:HD, :], ALU.mult)
                    q.then_inc(b_evacuated, 1)
                elif what == "key":
                    nc.vector.tensor_tensor(keysT[:, t % 2, NC + t // 2 * T:NC + t // 2 * T + T], src, rstd[:], ALU.mult).then_inc(b_evacuated, 1)
                if what == "key":
                    for kt in (2 * t, 2 * t + 1):
                        dve.wait_ge(gq_hi_done, kt + 1)
                        nc.vector.scalar_tensor_tensor(gq_lo[:, kt, :], x[:, kt, :], gain("mix1", kt), gq_hi[:, kt, :].bitcast(F32),
                                                       ALU.mult, ALU.subtract).then_inc(gq_lo_done, 1)
                if what == "gate":
                    dve.wait_ge(used_up, UB + b + 1)
                    nc.vector.scalar_tensor_tensor(backwards(gateT), bank[7][0:3 * HEADS, 0:T].rearrange("p (k t) -> p k t", k=2),
                                                   -1.0, rstd[0:3 * HEADS, :].rearrange("p (k t) -> p k t", k=2),
                                                   ALU.mult, ALU.mult).then_inc(gate_read, 1)
                if what == "w1" and t in (1, 3):
                    j = t // 2
                    dve.wait_ge(used_up, UB + b + 1)
                    z_j = gelu[:, 0, 60 * j:60 * j + 60]
                    nc.vector.tensor_scalar(z_j, hidden[j][:, 0:60], params[:, PAR["b1"] + j:PAR["b1"] + j + 1], None,
                                            ALU.add).then_inc(pre_gelu, 1)
                    dve.wait_ge(pre_gelu, 2 * j + 1)
                    nc.vector.tensor_tensor(z_j, z_j, hidden[j][:, 60:120], ALU.add).then_inc(pre_gelu, 1)
                if (what, t) == ("w1", 2):
                    dve.wait_ge(gate_turned, 1)
                    dve.wait_ge(consts_done, 6)
                    nc.vector.tensor_scalar(gate[:].rearrange("p k n -> p (k n)"), bank[7][:, T:T + 6 * HEADS], 1.0, None,
                                            ALU.add).then_inc(gate_step, 1)
                    dve.wait_ge(gate_step, 1)
                    nc.vector.reciprocal(gate[:], gate[:]).then_inc(gate_step, 1)
                    dve.wait_ge(gate_step, 2)
                    first = gate[:, 0, 0:3 * HEADS:3]
                    nc.vector.tensor_scalar(first, first, rowmask[:], None, ALU.mult).then_inc(gate_done, 1)
                z, a1, a2, th, hid = (gelu[:, n, :] for n in range(5))
                if (what, t) == ("w1", 3):
                    dve.wait_ge(pre_gelu, 4)
                    nc.vector.tensor_tensor(a1, z, z, ALU.mult).then_inc(gelu_step, 1)
                    dve.wait_ge(gelu_step, 1)
                    nc.vector.tensor_scalar(a1, a1, 0.044715, 1.0, ALU.mult, ALU.add).then_inc(gelu_step, 1)
                    dve.wait_ge(gelu_step, 2)
                    nc.vector.tensor_tensor(a2, a1, z, ALU.mult).then_inc(gelu_step, 1)
                if (what, t) == ("q", 2):
                    dve.wait_ge(gelu_tanh, 1)
                    nc.vector.tensor_scalar(th, th, 1.0, 0.5, ALU.add, ALU.mult).then_inc(gelu_step, 1)
                    dve.wait_ge(gelu_step, 4)
                    nc.vector.tensor_tensor(hid, th, z, ALU.mult).then_inc(hidden_done, 1)
                if what == "q":
                    query(t)
                if (what, t) == ("q", 3):
                    dve.wait_ge(cmp_mm, 1)
                    for p in range(2):
                        nc.vector.tensor_copy(keysT[HD * p:HD * p + HD, :, 0:NC],
                                              bank[6][0:HD, 128:128 + 60].rearrange("p (a q c) -> p a q c", a=2, q=2)[:, :, p, :])
                    nc.vector.tensor_copy(vc[:], bank[6][0:NC, 256:512]).then_inc(cmp_done, 1)
                rest("b", "up", b + AHEAD, 0)
                if (what, t) == ("q", Q_BEFORE - 1):
                    break
            dve.wait_ge(bias_landed, 16)
            dve.wait_ge(gate_done, 1)

            for e in range(HEADS + 4):
                if e < HEADS:
                    h = head_of(e)
                    r = e % 3
                    dve.wait_ge(scored, e + 1)
                    if e >= 3:
                        dve.wait_ge(turned1, e - 2)
                    s0, s1 = bank[2 * (e % 2)], bank[2 * (e % 2) + 1]
                    ends = bias[:, h, CL - 1::CS]
                    near, near_ends = bias[:, h, P:T], bias[:, h, P + CL - 1::CS]
                    slc_near, slc_far = s0[:, NC:NC + P], s1[:, P + NC:P + NC + T]
                    win_near, win_far = s1[:, 0:P], s0[:, NC + P:NC + P + T]
                    srcs = [(s0[:, 0:NC0], near_ends), (s1[:, P:P + NC], ends), (slc_near, near),
                            (slc_far, bias[:, h, :]), (win_near, near), (win_far, bias[:, h, :])]
                    for n, ((at, w), (sc, bi)) in enumerate(zip(SPANS, srcs)):
                        q = nc.vector.tensor_tensor_reduce(soft[:, r, at:at + w], sc, bi, -1.0, 3.0e38, ALU.add, ALU.min,
                                                           stats[:, r, n:n + 1])
                    q.then_inc(biased, 1)
                if e - 1 in Q_ROUND:
                    query(Q_ROUND[e - 1])
                    rest("b", "up", q_index(Q_ROUND[e - 1]) + AHEAD, 0)
                if e >= 5 and e % 2 == 1:
                    i = (e - 5) // 2
                    dve.wait_ge(o_hi_done, i + 1)
                    nc.vector.tensor_tensor(gx_lo[:, i, :].rearrange("p (k t) -> p k t", k=2), backwards(bank[6][:, 0:T]),
                                            gx_hi[:, i, :].bitcast(F32).rearrange("p (k t) -> p k t", k=2),
                                            ALU.subtract).then_inc(o_lo_done, 1)
                if 1 <= e < HEADS + 1:
                    g, r = e - 1, (e - 1) % 3
                    h = head_of(g)
                    dve.wait_ge(exped, g + 1)
                    nc.vector.reciprocal(stats[:, r, 12:18], stats[:, r, 6:12]).then_inc(recipd, 1)
                    dve.wait_ge(recipd, g + 1)
                    w = stats[:, r, 12:18].rearrange("p (b k) -> p b k", b=3)
                    nc.vector.tensor_tensor(w, w, gate[:, :, 3 * h:3 * h + 3].rearrange("p k b -> p b k"),
                                            ALU.mult).then_inc(weighted, 1)
                    dve.wait_ge(weighted, g + 1)
                    for n in WIDE:
                        at, w = SPANS[n]
                        q = nc.vector.tensor_scalar(soft[:, r, at:at + w], soft[:, r, at:at + w], stats[:, r, 12 + n:13 + n],
                                                    None, ALU.mult)
                    q.then_inc(normed_far, 1)
                if 2 <= e < HEADS + 2:
                    g = e - 2
                    dve.wait_ge(turned1, g + 1)
                    if g >= 2:
                        dve.wait_ge(headed, g - 1)
                    nc.vector.tensor_copy(probsT[:, g % 2, 512:768], bank[5][:, 0:T])
                    nc.vector.tensor_copy(probsT[0:NC, g % 2, 768:1024], bank[5][0:NC, T:2 * T]).then_inc(probs1, 1)
            for q in WHILE_O[:-1]:
                rest(*q)
            norm("f1", meanwhile=SOON("f1"))
            dve.wait_ge(padded, 2)
            stage("f1", [])
            norm("end")
            dve.wait_ge(x_gained, KT - 2)
            for b in range(3):
                nc.vector.tensor_tensor(x[:, 2 * b:2 * b + 2, :], x[:, 2 * b:2 * b + 2, :],
                                        rstd[:].unsqueeze(1).to_broadcast([P, 2, T]), ALU.mult).then_inc(out_done, 1)

        @block.tensor
        def _(pe):
            def three(out_ap, whi, wlo, xhi, xlo, start, stop):
                nc.tensor.matmul(out_ap, whi, xhi, start=start, stop=False, skip_group_check=True)
                nc.tensor.matmul(out_ap, whi, xlo, start=False, stop=False, skip_group_check=True)
                return nc.tensor.matmul(out_ap, wlo, xhi, start=False, stop=stop, skip_group_check=True)

            def product(q, dst, xh, xl, first, move=0, fresh=None, hi_sem=None):
                s = q["slot"]
                pe.wait_ge(lo_up, q["n"] + 1 + move)
                for kt in range(KT):
                    if fresh is not None:
                        pe.wait_ge(fresh, hi_sem + kt + 1)
                    mm = three(dst, w_hi[:, s, kt * P:kt * P + P], w_lo[:, s, kt * P:kt * P + P],
                               xh[:, kt, :], xl[:, kt, :], first and kt == 0, kt == KT - 1)
                mm.then_inc(used_up, 1)

            def up_place(st, k, c):
                if st == "a":
                    b, half = 2 * (k % 2) + c // 2, c % 2
                else:
                    b, half = UP[st] + k % 3, c
                return bank[b][:, half * T:(half + 1) * T], half == 0

            def up(st, k, i=0):
                fresh = (gx_lo_done, 8 * NORM[st]) if k == 0 else (None, None)
                ring = 2 if st == "a" else 3
                if k >= ring:
                    pe.wait_ge(scaled[st], k - ring + 1 + ring * i)
                move = stride(st, "up") * i
                for c in range(3 if st == "a" else 2):
                    dst, first = up_place(st, k, c)
                    product(piece_of(st, "up", k, c), dst, gx_hi, gx_lo, first, move, *fresh)

            def together(st, todo):
                for q, dst, first in todo:
                    pe.wait_ge(lo_up, q["n"] + 1)
                for kt in range(KT):
                    pe.wait_ge(gx_lo_done, 8 * NORM[st] + kt + 1)
                    if kt == KT - 1:
                        norm(st)
                    for q, dst, first in todo:
                        s = q["slot"]
                        mm = three(dst, w_hi[:, s, kt * P:kt * P + P], w_lo[:, s, kt * P:kt * P + P], gx_hi[:, kt, :],
                                   gx_lo[:, kt, :], first and kt == 0, kt == KT - 1)
                        if kt == KT - 1:
                            mm.then_inc(used_up, 1)

            def share(acc, first, last, s, yh, yl):
                for m in range(KT):
                    mm = three(bank[acc + m // 2][:, (m % 2) * T:(m % 2 + 1) * T], w_hi[:, s, m * P:m * P + P],
                               w_lo[:, s, m * P:m * P + P], yh, yl, first and m % 2 == 0, last)
                    if last and m in (1, 3, 5):
                        mm.then_inc(acc_done, 1)
                return mm

            def down(st, k, i=0):
                ring = 2 if st == "a" else 3
                r = k % ring
                q = piece_of(st, "down", k, 0)
                pe.wait_ge(y_lo_done[st], k + 1 + ring * i)
                pe.wait_ge(lo_down, q["n"] + 1 + stride(st, "down") * i)
                first = not looped(i) and k == 0
                last = not looped(i) and k == (AU if st == "a" else FU) - 1
                share(ACC[st], first, last, q["slot"], y_hi[:, r * T:(r + 1) * T], y_lo[:, r * T:(r + 1) * T]).then_inc(used_down, 1)

            def norm(st):
                k = NORM[st]
                if st == "end":
                    for b in range(4):
                        pe.wait_ge(squared, 4 * k + b + 1)
                        for h in range(2):
                            mm = nc.tensor.matmul(bank[NORM_BANK[st]][:, 0:T], ones[:], squares_end[b][:, h * T:h * T + T],
                                                  start=(b, h) == (0, 0), stop=(b, h) == (3, 1), skip_group_check=True)
                    mm.then_inc(norm_summed, 1)
                    return
                pe.wait_ge(summed, 2 * k + 2)
                pe.wait_ge(squared, 4 * k + 4)
                if k == 0:
                    pe.wait_ge(consts_done, 6)
                parts = [sumsq[:, 0, :], sumsq[:, 1, :], squares[:, 1, 0:T], squares[:, 1, T:2 * T]]
                for h, sq in enumerate(parts):
                    mm = nc.tensor.matmul(bank[NORM_BANK[st]][:, 0:T], ones[:], sq, start=h == 0, stop=h == 3, skip_group_check=True)
                if st == "b":
                    for t in range(2):
                        for h, sq in enumerate(parts):
                            mm = nc.tensor.matmul(bank[NORM_BANK[st]][:, T + t:T + t + 1], sq[:, t * P:t * P + P], ones[:, 0:1],
                                                  start=False, stop=h == 3, skip_group_check=True)
                mm.then_inc(norm_summed, 1)

            def stage(st):
                if st == "a":
                    up(st, 0)
                    norm(st)
                    pe.wait_ge(hot_landed, 32)
                    pe.wait_ge(table_done, 1)
                    nc.tensor.matmul(bank[4][0:HEADS, 0:384], table_sb, hot_sb[:, 0:384], start=True, stop=True).then_inc(rows_done, 1)
                    pe.wait_ge(deviated, 1)
                    up(st, 1)
                    for k in (2, 3):
                        up(st, k)
                        down(st, k - 2)
                    with pe.Fori(1, AU // 2 - 1) as i:
                        for k in (2, 3):
                            up(st, k, i)
                            down(st, k - 2, i)
                    down(st, AU - 2)
                    down(st, AU - 1)
                else:
                    together(st, [(piece_of(st, "up", k, c), *up_place(st, k, c)) for k in range(2) for c in range(2)])
                    up(st, 2)
                    down(st, 0)
                    with pe.Fori(0, ROUNDS) as i:
                        for k in (3, 4, 5):
                            up(st, k, i)
                            down(st, k - 2, i)
                    up(st, FU - 1)
                    for k in range(FU - 3, FU):
                        down(st, k)

            pe.wait_ge(consts_done, 1)
            for n in range(WARM):
                nc.tensor.matmul(bank[5][:, 0:P], ones[:], ones[:], start=True, stop=True)

            stage("a")
            stage("f0")

            UB = piece[("b", "up", 0, 0)]["n"]

            def queries(t):
                if t == 3:
                    pe.wait_ge(gate_done, 1)
                elif t > 3:
                    pe.wait_ge(b_evacuated, 8 + t)
                product(piece_of("b", "up", q_index(t), 0), q_bank(t), gq_hi, gq_lo, True)

            def compressed():
                pe.wait_ge(hidden_done, 1)
                hid = gelu[:, 4, :]
                w2 = params[:, PAR["w2"]:PAR["w2"] + 2 * HD]
                nc.tensor.matmul(bank[6][0:HD, 128:188], w2[:, 0:HD], hid[:, 0:60], start=True, stop=True)
                for g in range(GROUPS):
                    mm = nc.tensor.matmul(bank[6][0:NC, 256 + HD * g:256 + HD * g + HD], hid[:, 60 + NC * g:60 + NC * g + NC],
                                          w2[:, HD:2 * HD], start=True, stop=True)
                mm.then_inc(cmp_mm, 1)

            together("b", [(piece_of("b", "up", b, 0), pair_bank(b), b % 2 == 0) for b in range(4)])
            for b in range(4, q_index(Q_BEFORE - 1) + 1):
                what, t = B_ORDER[b]
                q = piece_of("b", "up", b, 0)
                s = q["slot"]
                if what == "key":
                    if b == 6:
                        pe.wait_ge(b_evacuated, 2)
                    product(q, pair_bank(b), gx_hi, gx_lo, b % 2 == 0)
                    continue
                if what == "q":
                    if t == 0:
                        pe.wait_ge(gq_lo_done, 8)
                        pe.wait_ge(b_evacuated, 8)
                    queries(t)
                    if t == 0:
                        pe.wait_ge(gate_exp, 1)
                        for k in range(2):
                            mm = nc.tensor.transpose(bank[7][:, T + 3 * HEADS * k:T + 3 * HEADS * (k + 1)],
                                                     gateT[:, k * P:k * P + P], ident[0:3 * HEADS, 0:3 * HEADS])
                        mm.then_inc(gate_turned, 1)
                    if t == Q_BEFORE - 2:
                        compressed()
                    continue
                pe.wait_ge(lo_up, q["n"] + 1)
                if what == "val":
                    if t == 0:
                        pe.wait_ge(x_new, 8)
                    for tt in range(2):
                        for kk in range(2):
                            kt = 2 * t + kk
                            mm = three(bank[4 + tt][:], gx_hi[:, kt, tt * P:tt * P + P], gx_lo[:, kt, tt * P:tt * P + P],
                                       w_hi[:, s, kk * 512:kk * 512 + 512], w_lo[:, s, kk * 512:kk * 512 + 512],
                                       kt == 0, kt == KT - 1)
                elif what == "w1":
                    j = t // 2
                    if t % 2 == 0:
                        pe.wait_ge(block_lo_done, j + 1)
                    for i8 in range(8):
                        i = 8 * (t % 2) + i8
                        nc.tensor.matmul(hidden[j][:, 0:120].rearrange("p (a n) -> p a n", a=2), w_hi[:, s, i8 * P:i8 * P + P],
                                         blocks[j][:, :, 60 * i:60 * i + 60], start=i == 0, stop=i == 15, skip_group_check=True)
                        mm = nc.tensor.matmul(hidden[j][:, 0:60], w_lo[:, s, i8 * P:i8 * P + P],
                                              blocks[j][:, 0, 60 * i:60 * i + 60], start=False, stop=i == 15, skip_group_check=True)
                elif what == "gate":
                    pe.wait_ge(gq_lo_done, 8)
                    for kt in range(KT):
                        mm = three(bank[7][0:3 * HEADS, 0:T], w_hi[:, s, 48 * kt:48 * kt + 48], w_lo[:, s, 48 * kt:48 * kt + 48],
                                   gq_hi[:, kt, :], gq_lo[:, kt, :], kt == 0, kt == KT - 1)
                mm.then_inc(used_up, 1)

            def scores(e):
                i, p = e // 2, e % 2
                a = i // HPG
                rows = slice(HD * p, HD * p + HD)
                s0, s1 = bank[2 * p], bank[2 * p + 1]
                pe.wait_ge(b_evacuated, 8 + max(i + 1, 2 + p))
                if e >= 2:
                    pe.wait_ge(biased, e - 1)
                near, far = (qT[rows, i, t * P:t * P + P] for t in range(2))
                beside = NC + P
                nc.tensor.matmul(s0[:, 0:beside], near, keysT[rows, a, 0:beside], start=True, stop=True)
                nc.tensor.matmul(s0[:, beside:beside + T], far, keysT[rows, a, NC + T:NC + 2 * T], start=True, stop=True)
                nc.tensor.matmul(s1[:, 0:P], near, keysT[rows, a, NC + T:NC + T + P], start=True, stop=True)
                nc.tensor.matmul(s1[:, P:P + NC + T], far, keysT[rows, a, 0:NC + T], start=True, stop=True).then_inc(scored, 1)

            def project(i):
                if i == 0:
                    pe.wait_ge(biased, HEADS)
                pe.wait_ge(o_lo_done, i + 1)
                q = piece_of("b", "up", O_FIRST + i, 0)
                pe.wait_ge(lo_up, q["n"] + 1)
                share(ACC["b"], i == 0, i == 7, q["slot"], gx_hi[:, i, :], gx_lo[:, i, :]).then_inc(used_up, 1)

            pe.wait_ge(cmp_done, 1)
            pe.wait_ge(vals_done, 2)
            scores(0)
            for e in range(HEADS + 3):
                if e + 1 < HEADS:
                    scores(e + 1)
                if 2 <= e < HEADS + 2:
                    g = e - 2
                    pe.wait_ge(normed, g + 1)
                    pe.wait_ge(normed_far, g + 1)
                    if g >= 1:
                        pe.wait_ge(probs0, g)
                    slc0, slc1, win0, win1 = (SPANS[n][0] for n in (2, 3, 4, 5))
                    for n, at in enumerate((slc0, slc1, win0, win1)):
                        mm = nc.tensor.transpose(bank[4][:, n * P:n * P + P], soft[:, g % 3, at:at + P], ident[:])
                    mm.then_inc(turned0, 1)
                    if g >= 1:
                        pe.wait_ge(probs1, g)
                    for n, at in enumerate((slc1, win1)):
                        nc.tensor.transpose(bank[5][:, n * P:n * P + P], soft[:, g % 3, at + P:at + T], ident[:])
                    if g == 0:
                        pe.wait_ge(zeroed, 1)
                    for n in range(2):
                        at = SPANS[n][0]
                        mm = nc.tensor.transpose(bank[5][0:NC, T + n * P:T + n * P + P], soft[:, g % 3, at:at + NC], ident[:])
                    mm.then_inc(turned1, 1)
                if e >= 3:
                    g = e - 3
                    i, p = g // 2, g % 2
                    grp = head_of(g) // HPG
                    pt = probsT[:, g % 2, :]
                    pe.wait_ge(probs0, g + 1)
                    pe.wait_ge(probs1, g + 1)
                    if p == 0 and i >= 1:
                        pe.wait_ge(o_lo_done, i)
                    dst = bank[6][HD * p:HD * p + HD, 0:T]
                    slc, win = (vals[:, :, n * T + HD * grp:n * T + HD * grp + HD] for n in range(2))
                    nc.tensor.matmul(dst, slc[:, 0], pt[:, 0:T], start=True, stop=False, skip_group_check=True)
                    nc.tensor.matmul(dst, win[:, 0], pt[:, T:2 * T], start=False, stop=False, skip_group_check=True)
                    nc.tensor.matmul(dst[:, P:T], slc[:, 1], pt[:, 512:640], start=False, stop=False, skip_group_check=True)
                    nc.tensor.matmul(dst[:, P:T], win[:, 1], pt[:, 640:768], start=False, stop=False, skip_group_check=True)
                    nc.tensor.matmul(dst, vc[:, HD * grp:HD * grp + HD], pt[0:NC, 768:1024], start=False, stop=True,
                                     skip_group_check=True).then_inc(headed, 1)
                if e in Q_ROUND:
                    queries(Q_ROUND[e])

                for i in O_ROUND.get(e, ()):
                    project(i)
            for i in range(sum(map(len, O_ROUND.values())), 8):
                project(i)
            stage("f1")
            norm("end")


SPANS = [(0, NC0), (16, NC), (32, P), (32 + P, T), (32 + P + T, P), (32 + 2 * P + T, T)]
NARROW, WIDE = (0, 1, 2, 4), (3, 5)


def head_of(e):
    i, p = e // 2, e % 2
    return (2 * (i // HPG) + p) * HPG + i % HPG


def backwards(ap):
    return ap.rearrange("p (k t) -> p k t", k=2)[:, :, ::-1]


NOTHING = ([], [], [])
AFTER_POOL = {("f0", "down", 0, 0), ("f0", "up", 2, 0), ("b", "up", 4, 0), ("f1", "down", 0, 0), ("f1", "up", 2, 0)}


def UPS(st, k, i=0):
    return [(st, "up", k, c, i) for c in range(3 if st == "a" else 2)]


def B_PIECES(a, b):
    return [("b", "up", k, 0) for k in range(a, b)]


def AHEAD_A(k, i=0):
    up = UPS("a", k + 2, i)
    return up[:1], up[1:], [("a", "down", k, 0, i)]


def AHEAD_F(st, k, i=0):
    up = UPS(st, k + 2, i)
    return up[:1], up[1:], [(st, "down", k + 1, 0, i)]


def SOON(st):
    return [(st, "down", 0, 0)] + UPS(st, 2)


WHILE_O = B_PIECES(NB - 2, NB) + UPS("f1", 0) + UPS("f1", 1)


def kernel(x, mix_norm, a_w_in, a_conv, a_w_out, ffn_norm, ffn_up, ffn_conv, ffn_down, kv_norm, w_kv, cmp_pe,
           cmp_w1, cmp_b1, cmp_w2, b_w_qg, b_w_o, rel_bias, final_norm):
    import concourse.bacc as bacc
    from concourse.bass_utils import run_bass_kernel_spmd as run

    c = lambda a: np.ascontiguousarray(np.asarray(a))
    tiles = lambda w, n: c(np.asarray(w).reshape(KT, P, n, P).transpose(2, 1, 0, 3)).reshape(n, P, PW)
    feat = lambda v: np.asarray(v).reshape(-1, P).T
    hd = HEADS * HD
    gains = np.concatenate([feat(v) for v in (mix_norm[0], ffn_norm[0], kv_norm, mix_norm[1], ffn_norm[1], final_norm)], 1)
    a_taps = np.asarray(a_conv)[0].reshape(3, AU, P).transpose(2, 1, 0).reshape(P, -1)
    f_taps = np.asarray(ffn_conv).reshape(2, 3, 2 * FU, P).transpose(3, 0, 2, 1).reshape(P, -1)
    pe = np.asarray(cmp_pe).reshape(2, 16, P).transpose(2, 0, 1).reshape(P, -1)
    w2 = np.asarray(cmp_w2).transpose(1, 0, 2).reshape(P, -1)
    par = np.concatenate([gains, a_taps, f_taps, pe, np.asarray(cmp_b1).T, w2], 1)
    a_up = tiles(np.asarray(a_w_in)[0], 3 * AU).reshape(3, AU, P, PW).transpose(1, 0, 2, 3)
    f_up = np.stack([tiles(w, 2 * FU).reshape(2, FU, P, PW).transpose(1, 0, 2, 3) for w in np.asarray(ffn_up)])
    kv = np.asarray(w_kv).reshape(D, 6, GROUPS * HD)
    kv_tiles = lambda s: list(tiles(kv[:, s], 2))
    val = np.concatenate([kv[:, 3], kv[:, 5]], 1).reshape(4, 2, P, 512).transpose(0, 2, 1, 3).reshape(4, P, PW)
    w1 = np.asarray(cmp_w1).reshape(2, 2, 8, P, P).transpose(0, 1, 3, 2, 4).reshape(4, P, PW)
    qg = np.asarray(b_w_qg)[0]
    heads = [head_of(e) for e in range(HEADS)]
    q = tiles(qg[:, :hd].reshape(D, HEADS, HD)[:, heads].reshape(D, hd), 8)
    g = np.zeros((P, PW), qg.dtype)
    g[:, :8 * 3 * HEADS] = qg[:, hd:].reshape(KT, P, 3 * HEADS).transpose(1, 0, 2).reshape(P, -1)
    sets = {"cmp": kv_tiles(0) + kv_tiles(1), "key": kv_tiles(2) + kv_tiles(4), "val": list(val), "w1": list(w1),
            "gate": [g], "q": list(q)}
    b_up = np.stack([sets[what][t] for what, t in B_ORDER[:O_FIRST]])
    b_down = np.asarray(b_w_o)[0].reshape(HEADS, HD, D)[heads].reshape(8, P, PW)
    arrays = {
        "xT": np.asarray(x)[0].T.reshape(KT, P, T).transpose(1, 0, 2), "par": par, "hot": one_hot_of_distances(),
        "rel": rel_bias, "a_up": a_up, "a_down": np.asarray(a_w_out)[0].reshape(AU, P, PW), "f_up": f_up,
        "f_down": np.asarray(ffn_down).reshape(2, FU, P, PW), "b_up": b_up, "b_down": b_down,
    }
    arrays = {k: c(v) for k, v in arrays.items()}
    nc = bacc.Bacc("TRN2", target_bir_lowering=False, num_devices=1)
    args = [nc.dram_tensor(f"in_{k}", v.shape, F32, kind="ExternalInput").ap() for k, v in arrays.items()]
    scratch = nc.dram_tensor("bias_rows", [HEADS, 384], F32, kind="Internal").ap()
    out = nc.dram_tensor("out", (P, KT, T), F32, kind="ExternalOutput").ap()
    build(nc, *args, scratch, out)
    r = run(nc, [{f"in_{k}": v for k, v in arrays.items()}], core_ids=[0])
    return c(r.results[0]["out"].transpose(2, 1, 0)).reshape(1, T, D)
```
